# Optimizing a Trainium2 kernel written in Bass

```python
import jax, jax.numpy as jnp
from jax import lax
import numpy as np

D_MODEL = 2048
BATCH = 1
SEQ = 256
DEPTH = 1

MEM_LEN = 256
FOX_HEADS = 8
FOX_HEAD_DIM = 128
FOX_WIDTH = FOX_HEADS * FOX_HEAD_DIM
MLSTM_HEADS = 4
MLSTM_HEAD_DIM = 256
MLSTM_WIDTH = MLSTM_HEADS * MLSTM_HEAD_DIM
MEM_HEADS = 4
MEM_HEAD_DIM = 256
MEM_WIDTH = MEM_HEADS * MEM_HEAD_DIM
N_BRANCH = 3
CONV_WIDTH = 4
Q_BLOCK = 128
CHUNK = 128
D_FF = -(-8 * D_MODEL // (3 * 256)) * 256
EPS = 1e-6
FOX_FORGET_BIAS_LO = 1.0
FOX_FORGET_BIAS_HI = 5.0
MLSTM_FORGET_BIAS_LO = 3.0
MLSTM_FORGET_BIAS_HI = 6.0

IN_SIZES = (FOX_WIDTH, FOX_WIDTH, FOX_WIDTH, FOX_HEADS,
            MLSTM_WIDTH, MLSTM_WIDTH, MLSTM_WIDTH, MLSTM_HEADS, MLSTM_HEADS, MLSTM_WIDTH,
            MEM_WIDTH, N_BRANCH * D_MODEL)
IN_SPLITS = tuple(sum(IN_SIZES[:i + 1]) for i in range(len(IN_SIZES) - 1))
PROJ_WIDTH = sum(IN_SIZES)
FOX_F_OFF = sum(IN_SIZES[:3])
MLSTM_F_OFF = sum(IN_SIZES[:8])

kernel_name = "hybrid_fox_mlstm_memxattn_gated"

def rmsnorm(x, g):
    xf = x.astype(jnp.float32)
    y = xf * lax.rsqrt(jnp.mean(xf * xf, axis=-1, keepdims=True) + EPS)
    return (y * g.astype(jnp.float32)).astype(x.dtype)

def split_heads(t, n):
    b, s, w = t.shape
    return t.reshape(b, s, n, w // n).transpose(0, 2, 1, 3)

def merge_heads(t):
    b, h, s, d = t.shape
    return t.transpose(0, 2, 1, 3).reshape(b, s, h * d)

def causal_depthwise_conv(x, w, bias):
    k = w.shape[0]
    y = lax.conv_general_dilated(x, w[:, None, :], window_strides=(1,), padding=[(k - 1, 0)],
                                 dimension_numbers=('NWC', 'WIO', 'NWC'),
                                 feature_group_count=x.shape[-1])
    return y + bias

def forgetting_attention(q, k, v, log_f):
    b, h, s, dh = q.shape
    nb = s // Q_BLOCK
    F = jnp.cumsum(log_f, axis=-1)
    qb = q.reshape(b, h, nb, Q_BLOCK, dh).transpose(2, 0, 1, 3, 4)
    Fb = F.reshape(b, h, nb, Q_BLOCK).transpose(2, 0, 1, 3)
    kpos = jnp.arange(s)
    scale = dh ** -0.5

    def block(args):
        qi, Fi, i = args
        qpos = i * Q_BLOCK + jnp.arange(Q_BLOCK)
        logits = (jnp.einsum('bhqd,bhkd->bhqk', qi, k) * scale
                  + Fi[..., :, None] - F[..., None, :])
        logits = jnp.where(kpos[None, :] <= qpos[:, None], logits, -jnp.inf)
        p = jax.nn.softmax(logits, axis=-1)
        return jnp.einsum('bhqk,bhkd->bhqd', p, v)

    out = lax.map(block, (qb, Fb, jnp.arange(nb)))
    return out.transpose(1, 2, 0, 3, 4).reshape(b, h, s, dh)

def mlstm_chunkwise(q, k, v, i_pre, log_f):
    b, h, s, dk = q.shape
    dv = v.shape[-1]
    nc = s // CHUNK

    def chunks(a):
        return jnp.moveaxis(a.reshape(b, h, nc, CHUNK, *a.shape[3:]), 2, 0)

    causal = jnp.tril(jnp.ones((CHUNK, CHUNK), dtype=bool))

    def step(carry, xs):
        C, n, m = carry
        qj, kj, vj, ij, fj = xs
        bcum = jnp.cumsum(fj, axis=-1)
        dlog = bcum[..., :, None] - bcum[..., None, :] + ij[..., None, :]
        dlog = jnp.where(causal, dlog, -jnp.inf)
        inter = bcum + m[..., None]
        m_t = jnp.maximum(inter, jnp.max(dlog, axis=-1))
        w = jnp.exp(dlog - m_t[..., None])
        a = jnp.exp(inter - m_t)
        qk = jnp.einsum('bhtd,bhsd->bhts', qj, kj) * w
        num = (a[..., None] * jnp.einsum('bhtd,bhde->bhte', qj, C)
               + jnp.einsum('bhts,bhse->bhte', qk, vj))
        den = a * jnp.einsum('bhtd,bhd->bht', qj, n) + jnp.sum(qk, axis=-1)
        h_out = num / jnp.maximum(jnp.abs(den), jnp.exp(-m_t))[..., None]
        b_end = bcum[..., -1]
        g = b_end[..., None] - bcum + ij
        m_new = jnp.maximum(b_end + m, jnp.max(g, axis=-1))
        decay = jnp.exp(b_end + m - m_new)
        ws = jnp.exp(g - m_new[..., None])
        C_new = decay[..., None, None] * C + jnp.einsum('bhs,bhsd,bhse->bhde', ws, kj, vj)
        n_new = decay[..., None] * n + jnp.einsum('bhs,bhsd->bhd', ws, kj)
        return (C_new, n_new, m_new), h_out

    init = (jnp.zeros((b, h, dk, dv), jnp.float32), jnp.zeros((b, h, dk), jnp.float32),
            jnp.zeros((b, h), jnp.float32))
    _, hs = lax.scan(step, init, (chunks(q), chunks(k), chunks(v), chunks(i_pre), chunks(log_f)))
    return jnp.moveaxis(hs, 0, 2).reshape(b, h, s, dv)

def head_rmsnorm(t, g):
    y = t * lax.rsqrt(jnp.mean(t * t, axis=-1, keepdims=True) + EPS)
    return merge_heads(y) * g.astype(jnp.float32)

def memory_attention(q, mk, mv):
    logits = jnp.einsum('bhqd,bhmd->bhqm', q, mk) * (q.shape[-1] ** -0.5)
    p = jax.nn.softmax(logits, axis=-1)
    return jnp.einsum('bhqm,bhmd->bhqd', p, mv)

def setup_inputs(seed: int = 0) -> dict:
    key = jax.random.key(seed)
    ks = jax.random.split(key, 20)
    nrm = lambda k, shape: jax.random.normal(k, shape, jnp.float32)
    x = nrm(ks[0], (BATCH, SEQ, D_MODEL))
    mem = nrm(ks[1], (BATCH, MEM_LEN, D_MODEL))
    norm_mix = 1.0 + 0.02 * nrm(ks[2], (DEPTH, D_MODEL))
    w_in = nrm(ks[3], (DEPTH, D_MODEL, PROJ_WIDTH)) * D_MODEL ** -0.5
    b_in = 0.01 * nrm(ks[4], (DEPTH, PROJ_WIDTH))
    b_in = b_in.at[:, FOX_F_OFF:FOX_F_OFF + FOX_HEADS].add(
        jnp.linspace(FOX_FORGET_BIAS_LO, FOX_FORGET_BIAS_HI, FOX_HEADS))
    b_in = b_in.at[:, MLSTM_F_OFF:MLSTM_F_OFF + MLSTM_HEADS].add(
        jnp.linspace(MLSTM_FORGET_BIAS_LO, MLSTM_FORGET_BIAS_HI, MLSTM_HEADS))
    conv_w = nrm(ks[5], (DEPTH, CONV_WIDTH, 2 * MLSTM_WIDTH)) * CONV_WIDTH ** -0.5
    conv_b = 0.01 * nrm(ks[6], (DEPTH, 2 * MLSTM_WIDTH))
    mlstm_norm = 1.0 + 0.02 * nrm(ks[7], (DEPTH, MLSTM_WIDTH))
    norm_mem = 1.0 + 0.02 * nrm(ks[8], (DEPTH, D_MODEL))
    w_mem_kv = nrm(ks[9], (DEPTH, D_MODEL, 2 * MEM_WIDTH)) * D_MODEL ** -0.5
    w_br_fox = nrm(ks[10], (DEPTH, FOX_WIDTH, D_MODEL)) * FOX_WIDTH ** -0.5
    w_br_mlstm = nrm(ks[11], (DEPTH, MLSTM_WIDTH, D_MODEL)) * MLSTM_WIDTH ** -0.5
    w_br_mem = nrm(ks[12], (DEPTH, MEM_WIDTH, D_MODEL)) * MEM_WIDTH ** -0.5
    w_out = nrm(ks[13], (DEPTH, D_MODEL, D_MODEL)) * D_MODEL ** -0.5
    norm_ffn = 1.0 + 0.02 * nrm(ks[14], (DEPTH, D_MODEL))
    w_ffn_in = nrm(ks[15], (DEPTH, D_MODEL, 2 * D_FF)) * D_MODEL ** -0.5
    w_ffn_out = nrm(ks[16], (DEPTH, D_FF, D_MODEL)) * D_FF ** -0.5
    norm_final = 1.0 + 0.02 * nrm(ks[17], (D_MODEL,))
    return {"x": x, "mem": mem, "norm_mix": norm_mix, "w_in": w_in, "b_in": b_in,
            "conv_w": conv_w, "conv_b": conv_b, "mlstm_norm": mlstm_norm,
            "norm_mem": norm_mem, "w_mem_kv": w_mem_kv, "w_br_fox": w_br_fox,
            "w_br_mlstm": w_br_mlstm, "w_br_mem": w_br_mem, "w_out": w_out,
            "norm_ffn": norm_ffn, "w_ffn_in": w_ffn_in, "w_ffn_out": w_ffn_out,
            "norm_final": norm_final}

def reference(x, mem, norm_mix, w_in, b_in, conv_w, conv_b, mlstm_norm, norm_mem, w_mem_kv,
              w_br_fox, w_br_mlstm, w_br_mem, w_out, norm_ffn, w_ffn_in, w_ffn_out, norm_final):
    f32 = jnp.float32
    h = x
    bsz, seq, _ = x.shape
    for l in range(DEPTH):
        u = rmsnorm(h, norm_mix[l])
        proj = u @ w_in[l] + b_in[l]
        (fq, fk, fv, ff, lq, lk, lv, li, lf, lo, mq, gates) = jnp.split(proj, IN_SPLITS, axis=-1)

        fox_logf = jax.nn.log_sigmoid(ff.astype(f32)).transpose(0, 2, 1)
        y_fox = forgetting_attention(split_heads(fq, FOX_HEADS).astype(f32),
                                     split_heads(fk, FOX_HEADS).astype(f32),
                                     split_heads(fv, FOX_HEADS).astype(f32), fox_logf)
        y_fox = merge_heads(y_fox).astype(x.dtype)

        qk_in = jax.nn.silu(causal_depthwise_conv(jnp.concatenate([lq, lk], axis=-1),
                                                  conv_w[l], conv_b[l]))
        lq_c, lk_c = jnp.split(qk_in, 2, axis=-1)
        h_ml = mlstm_chunkwise(split_heads(lq_c, MLSTM_HEADS).astype(f32),
                               split_heads(lk_c, MLSTM_HEADS).astype(f32) * (MLSTM_HEAD_DIM ** -0.5),
                               split_heads(lv, MLSTM_HEADS).astype(f32),
                               li.astype(f32).transpose(0, 2, 1),
                               jax.nn.log_sigmoid(lf.astype(f32)).transpose(0, 2, 1))
        y_ml = (head_rmsnorm(h_ml, mlstm_norm[l]) * jax.nn.sigmoid(lo.astype(f32))).astype(x.dtype)

        mkv = rmsnorm(mem, norm_mem[l]) @ w_mem_kv[l]
        mk, mv = jnp.split(mkv, 2, axis=-1)
        y_mem = memory_attention(split_heads(mq, MEM_HEADS).astype(f32),
                                 split_heads(mk, MEM_HEADS).astype(f32),
                                 split_heads(mv, MEM_HEADS).astype(f32))
        y_mem = merge_heads(y_mem).astype(x.dtype)

        g = jax.nn.sigmoid(gates.astype(f32)).astype(x.dtype).reshape(bsz, seq, N_BRANCH, D_MODEL)
        merged = (g[:, :, 0] * (y_fox @ w_br_fox[l])
                  + g[:, :, 1] * (y_ml @ w_br_mlstm[l])
                  + g[:, :, 2] * (y_mem @ w_br_mem[l]))
        h = h + merged @ w_out[l]

        u = rmsnorm(h, norm_ffn[l])
        gate_ff, up_ff = jnp.split(u @ w_ffn_in[l], 2, axis=-1)
        h = h + (jax.nn.silu(gate_ff) * up_ff) @ w_ffn_out[l]
    return rmsnorm(h, norm_final)


_drawn_inputs = setup_inputs


def setup_inputs(seed=0):
    import zlib

    import numpy as np

    out = dict(_drawn_inputs(seed))
    spreads = {}
    factors = {'norm_mix': 4.766,
     'conv_b': 200.0,
     'mlstm_norm': 93.992,
     'norm_mem': 8.0,
     'norm_ffn': 13.632,
     'norm_final': 22.557}
    for name, (base, spread) in spreads.items():
        noise = np.random.default_rng([zlib.crc32(name.encode()), seed]).standard_normal(out[name].shape)
        drawn = base * np.exp(spread * noise) if base else spread * noise
        out[name] = __import__('jax').numpy.asarray(drawn.astype(out[name].dtype))
    for name, factor in factors.items():
        out[name] = (out[name] * factor).astype(out[name].dtype)
    return out
```

```python
from contextlib import ExitStack

import concourse.bass as bass
from concourse import mybir

F32 = mybir.dt.float32
F32R = mybir.dt.float32r
ALU = mybir.AluOpType
ACT = mybir.ActivationFunctionType
AX_X = mybir.AxisListType.X

P = 128
SEQ = 256
TT = SEQ // P
D = 2048
KD = D // P
NCOL = 512
UK = 2
NT = D // NCOL
EPS = 1e-6
MEM_LEN = 256
FOX_H, FOX_D = 8, 128
ML_H, ML_D = 4, 256
MEM_H, MEM_D = 4, 256
W = 1024
KW = W // P
D_FF = -(-8 * D // (3 * 256)) * 256
FT = D_FF // NCOL
FT_A = (FT + 1) // 2
RING = 4
LEAD = RING - 1
GROUPS = 4
GC = W // GROUPS

FOX_Q, FOX_F = 0, 3 * W
ML_Q = FOX_F + FOX_H
ML_V = ML_Q + 2 * W
ML_I = ML_Q + 3 * W
ML_O = ML_I + 2 * ML_H
MEM_Q = ML_O + W
GATES = MEM_Q + W
SMALL = FOX_H + 2 * ML_H


class Job:

    def __init__(self, lhs, kts, width, loads=1):
        self.lhs, self.kts, self.width, self.loads = lhs, kts, width, loads
        self.units = kts // UK


class Phase:
    def __init__(self, name, jobs, iters):
        self.name, self.jobs, self.iters = name, jobs, iters
        self.units = [(j, k) for j, job in enumerate(jobs) for k in range(job.units)]


def phases():
    out = [
        Phase("mem", [Job("mem", KD, NCOL, 2), Job("u", KD, GC)], GROUPS),
        Phase("ml", [Job("u", KD, NCOL, 2), Job("u", KD, NCOL, 2)], GROUPS),
        Phase("fox", [Job("u", KD, NCOL, 2), Job("u", KD, GC)], GROUPS),
        Phase("merge", [Job("u", KD, NCOL, 2), Job("y_mem", KW, NCOL), Job("u", KD, NCOL),
                        Job("y_ml", KW, NCOL), Job("u", KD, NCOL), Job("y_fox", KW, NCOL)], NT),
        Phase("out", [Job("merged", KD, NCOL, 2)] + [Job("merged", KD, NCOL)] * (NT - 1), 1),
        Phase("ffn_a", [Job("u", KD, NCOL), Job("u", KD, NCOL)], FT_A),
        Phase("down_a", [Job("hidden", FT_A * NCOL // P, NCOL)] * NT, 1),
        Phase("ffn_b", [Job("u", KD, NCOL), Job("u", KD, NCOL)], FT - FT_A),
        Phase("down_b", [Job("hidden", (FT - FT_A) * NCOL // P, NCOL)] * NT, 1),
    ]
    unit = job = 0
    loads = [0] * RING
    for p in out:
        p.unit0, p.job0, p.loads0 = unit, job, list(loads)
        p.per_slot = [sum(p.jobs[j].loads for j, _ in p.units[s::RING]) for s in range(RING)]
        loads = [a + b * p.iters for a, b in zip(loads, p.per_slot)]
        unit += len(p.units) * p.iters
        job += len(p.jobs) * p.iters
        assert len(p.units) % RING == 0 and len(p.jobs) % 2 == 0
    for p, q in zip(out, out[1:]):
        assert p.iters == 1 or p.jobs[0].loads == q.jobs[0].loads
    return out, unit


PHASES, UNITS = phases()
PHASE = {p.name: p for p in PHASES}

LINKS = {"mem": 2, "ml": 8, "fox": 5, "merge": 6, "ffn_a": 0, "ffn_b": 0}


class Chain:

    def __init__(self, engine, sem, links):
        self.engine, self.sem, self.links, self.n, self.turn = engine, sem, links, 0, None

    def link(self, instruction):
        instruction.then_inc(self.sem, 1)
        self.n += 1
        value = self.n if self.turn is None else self.turn + self.n
        self.engine.wait_ge(self.sem, value)

    def enter(self, i, first, phase):
        self.per = self.links[phase]
        self.turn, self.at = (i - first) * self.per, self.n

    def leave(self, turns):
        assert self.n - self.at == self.per, (self.n - self.at, self.per)
        self.n, self.turn = self.at + self.per * turns, None


def peeled(i):
    return isinstance(i, int)


def run_phases(engine, iteration, chain=None):
    for prev, phase in zip([None] + PHASES, PHASES):
        iteration(phase, 0, prev)
        if phase.iters > 1:
            with engine.Fori(1, phase.iters) as i:
                if chain:
                    chain.enter(i, 1, phase.name)
                iteration(phase, i, phase)
            if chain:
                chain.leave(phase.iters - 1)


def hybrid_layer(nc, x, mem, norm_mix, w_in, b_in, conv_w, conv_b, mlstm_norm, norm_mem, w_mem_kv,
                 w_br_fox, w_br_mlstm, w_br_mem, w_out, norm_ffn, w_ffn_in, w_ffn_out, norm_final, out):
    ctx = ExitStack()
    place = [(nc.sbuf_base + 63) // 64 * 64]

    def at(name, shape, dt, offset):
        return nc.alloc_sbuf_tensor_at(name, shape, dt, offset=offset)

    def sb(name, shape, dt=F32):
        size = 4
        for s in shape[1:]:
            size *= s
        offset = place[0]
        place[0] += (size + 31) // 32 * 32
        assert place[0] <= nc.sbuf_top, (name, place[0])
        return at(name, shape, dt, offset)

    with ctx:
        def sem(name):
            return ctx.enter_context(nc.semaphore(name))

        w_raw = sb("w_raw", [P, RING, UK, NCOL])
        w_hi = sb("w_hi", [P, RING, UK, NCOL], F32R)
        w_lo = sb("w_lo", [P, RING, UK, NCOL], F32R)
        bias = sb("bias", [P, 2, NCOL])

        u_hi = sb("u_hi", [P, KD, SEQ], F32R)
        u_lo = sb("u_lo", [P, KD, SEQ], F32R)
        region_b = place[0]
        mem_hi = sb("mem_hi", [P, KD, SEQ], F32R)
        mem_lo = sb("mem_lo", [P, KD, SEQ], F32R)
        region_c = place[0]
        y = {}
        for b in ("mem", "ml", "fox"):
            y[b] = (sb(f"y_{b}_hi", [P, KW, SEQ], F32R), sb(f"y_{b}_lo", [P, KW, SEQ], F32R))
        KB = 1024
        merged_hi = at("merged_hi", [P, KD, SEQ], F32R, region_b)
        merged_lo = at("merged_lo", [P, KD, SEQ], F32R, region_b + 16 * KB)
        squares = at("squares", [P, D], F32, region_c)
        mem_in = at("mem_in", [P, TT, D], F32, region_c + 16 * KB)
        x_in = at("x_in", [P, TT, D], F32, region_c + 32 * KB)
        res = at("res", [P, TT, D], F32, region_c)
        h_hi = at("h_hi", [P, FT_A * NCOL // P, SEQ], F32R, region_c + 16 * KB)
        h_lo = at("h_lo", [P, FT_A * NCOL // P, SEQ], F32R, region_b)
        g_final = at("g_final", [P, D], F32, region_c + 40 * KB)
        lhs = {"mem": (mem_hi, mem_lo), "u": (u_hi, u_lo), "merged": (merged_hi, merged_lo),
               "hidden": (h_hi, h_lo), "y_mem": y["mem"], "y_ml": y["ml"], "y_fox": y["fox"]}

        buf_a = sb("buf_a", [P, TT, NCOL])
        buf_b = sb("buf_b", [P, TT, 2, GC + 4])
        buf_x = sb("buf_x", [P, 4, SEQ + 4])
        buf_p = sb("buf_p", [P, 4, SEQ])
        buf_t = sb("buf_t", [P, 4, SEQ])
        buf_y = sb("buf_y", [P, TT, GC])
        buf_f = sb("buf_f", [FOX_H, 2, SEQ])
        region_g = place[0]
        gate = sb("gate", [P, TT, NCOL])
        region_m = place[0]
        merged = sb("merged", [P, TT, NCOL])
        scratch = sb("scratch", [P, NCOL])

        small_raw = at("small_raw", [P, KD, SMALL], F32, region_g)
        small_hi = at("small_hi", [P, KD, SMALL], F32R, region_g + KB)
        small_lo = at("small_lo", [P, KD, SMALL], F32R, region_g + 2 * KB)
        ones_row = at("ones_row", [FOX_H, SEQ], F32, region_m)
        f_ml = at("f_ml", [ML_H, SEQ], F32, region_m + KB)
        a_ml = at("a_ml", [ML_H, SEQ], F32, region_m + 2 * KB)
        fm_ml = at("fm_ml", [ML_H, SEQ], F32, region_m + 3 * KB)
        f_fox = sb("f_fox", [FOX_H, SEQ])
        m_ml = sb("m_ml", [ML_H, SEQ])
        small_bias = sb("small_bias", [P, SMALL])
        z = sb("z", [P, TT, SMALL])
        z_abs = sb("z_abs", [P, TT, SMALL])
        log_sig = sb("log_sig", [P, TT, SMALL])
        a_col = sb("a_col", [P, TT, ML_H])
        floor_col = sb("floor_col", [P, TT, ML_H])

        ident = sb("ident", [P, P])
        mask_add = sb("mask_add", [P, 3, P])
        mask_mul = sb("mask_mul", [P, P])
        minus_one = sb("minus_one", [FOX_H, P])
        plus_one = sb("plus_one", [ML_H, P])
        eps = sb("eps", [P, 1])
        vec_rows = sb("vec_rows", [P, P])
        vec = sb("vec", [P, P])
        ml_rows = sb("ml_rows", [KW, P])
        ml_gain = sb("ml_gain", [P, KW])
        V_MIX, V_MEM, V_FFN, V_CB, V_CW = 0, KD, 2 * KD, 3 * KD, 4 * KD
        ssq = sb("ssq", [P, 4, TT, NT])
        rstd = sb("rstd", [P, 4, TT])
        stat = sb("stat", [P, 4, 4])

        acc = ctx.enter_context(nc.psum_tensor("acc", [P, 4, NCOL], F32))
        att = ctx.enter_context(nc.psum_tensor("att", [P, 4, NCOL], F32))

        raw_full = [sem(f"raw_full{s}") for s in range(RING)]
        hi_done, split_done, unit_used = sem("hi_done"), sem("split_done"), sem("unit_used")
        acc_read = sem("acc_read")
        bias_full = [sem("bias_full0"), sem("bias_full1")]
        consts, vecs_in, vecs_turned, vecs_done = sem("consts"), sem("vecs_in"), sem("vecs_turned"), sem("vecs_done")
        mem_here, x_here, small_here, small_bias_here, res_here, final_here = (
            sem("mem_here"), sem("x_here"), sem("small_here"), sem("small_bias_here"), sem("res_here"), sem("final_here"))
        start_turned, start_hi, start_lo = sem("start_turned"), sem("start_hi"), sem("start_lo")
        squared, mean_sq, rooted, rstd_done = sem("squared"), sem("mean_sq"), sem("rooted"), sem("rstd_done")
        small_hi_done, small_split, small_mm, small_act, small_dve, small_pe = (
            sem("small_hi_done"), sem("small_split"), sem("small_mm"), sem("small_act"), sem("small_dve"),
            sem("small_pe"))
        step_pe = {b: sem(f"{b}_step_pe") for b in ("mem", "ml", "fox")}
        step_dve = {b: sem(f"{b}_step_dve") for b in ("mem", "ml", "fox")}
        step_act = {b: sem(f"{b}_step_act") for b in ("mem", "ml", "fox")}
        y_hi = {b: sem(f"{b}_y_hi") for b in ("mem", "ml", "fox")}
        y_done = {b: sem(f"{b}_y_done") for b in ("mem", "ml", "fox")}
        gate_done = sem("gate_done")
        tile_turned, tile_hi, tile_lo = sem("tile_turned"), sem("tile_hi"), sem("tile_lo")
        ffn_sig, final_done, stored = sem("ffn_sig"), sem("final_done"), sem("stored")
        dve_order, pool_order = sem("dve_order"), sem("pool_order")
        block = ctx.enter_context(nc.Block())

        PE_STEPS = {"mem": 4, "ml": 4, "fox": 5}
        DVE_STEPS = {"mem": 4, "ml": 6, "fox": 5}
        ACT_STEPS = {"mem": 3, "ml": 7, "fox": 4}

        TILE0 = {"merge": 0, "out": NT, "ffn_a": 2 * NT, "ffn_b": 2 * NT + FT_A}

        def iteration_units(phase, i):
            for u, (j, k) in enumerate(phase.units):
                yield i * len(phase.units) + (phase.unit0 + u), u % RING, u, j, phase.jobs[j], k

        def job_number(phase, i, j):
            return i * len(phase.jobs) + (phase.job0 + j)

        def pair(w, first, step, i, rows):
            v = w[:, first:first + 2 * step].rearrange("(k p) (g c) -> p k g c", p=P, g=2)
            return v[:, rows, :, bass.ds(i * GC, GC)]

        def flat(w, cols, rows):
            return w.rearrange("(k p) c -> p k c", p=P)[:, rows, cols]

        def source(phase, i, j, k):
            rows = slice(k * UK, (k + 1) * UK)
            if phase.name == "mem":
                return pair(w_mem_kv[0], 0, W, i, rows) if j == 0 else \
                    flat(w_in[0], bass.ds(i * GC + MEM_Q, GC), rows)
            if phase.name == "ml":
                return pair(w_in[0], ML_Q, W, i, rows) if j == 0 else pair(w_in[0], ML_V, ML_O - ML_V, i, rows)
            if phase.name == "fox":
                return pair(w_in[0], FOX_Q, W, i, rows) if j == 0 else \
                    flat(w_in[0], bass.ds(i * GC + 2 * W, GC), rows)
            if phase.name == "merge":
                b = 2 - j // 2
                if j % 2 == 0:
                    return flat(w_in[0], bass.ds(i * NCOL + (GATES + b * D), NCOL), rows)
                return flat((w_br_fox, w_br_mlstm, w_br_mem)[b][0], bass.ds((i - 1) * NCOL + NCOL, NCOL), rows)
            if phase.name == "out":
                return flat(w_out[0], slice(j * NCOL, (j + 1) * NCOL), rows)
            tile0 = 0 if phase.name.endswith("a") else FT_A
            if phase.name.startswith("ffn"):
                return flat(w_ffn_in[0], bass.ds(i * NCOL + (tile0 * NCOL + j * D_FF), NCOL), rows)
            kt0 = tile0 * NCOL // P
            rows = slice(kt0 + k * UK, kt0 + (k + 1) * UK)
            return flat(w_ffn_out[0], slice(j * NCOL, (j + 1) * NCOL), rows)

        def bias_of(phase, j):
            if phase.name == "mem":
                return (1, 0, 1) if j == 1 else None
            if phase.name in ("ml", "fox"):
                return (j, 0, 1)
            if phase.name == "merge" and j % 2 == 0:
                return ((j // 2) % 2, j // 4, 2 - (j // 2) % 2)
            return None

        BIAS0 = {"mem": (0, 0), "ml": (0, GROUPS), "fox": (GROUPS, 2 * GROUPS), "merge": (2 * GROUPS, 3 * GROUPS)}

        def bias_number(phase, i, j):
            slot, k, per = bias_of(phase, j)
            return slot, i * per + (BIAS0[phase.name][slot] + k)

        def bias_source(phase, i, j):
            b = b_in[0]
            if phase.name == "mem":
                v = b[bass.ds(i * GC + MEM_Q, GC)]
            elif phase.name == "merge":
                v = b[bass.ds(i * NCOL + (GATES + (2 - j // 2) * D), NCOL)]
            elif phase.name == "fox" and j == 1:
                v = b[bass.ds(i * GC + 2 * W, GC)]
            else:
                first, step = ((FOX_Q, W) if phase.name == "fox" else (ML_Q, W) if j == 0 else (ML_V, ML_O - ML_V))
                v = b[first:first + 2 * step].rearrange("(g c) -> g c", g=2)[:, bass.ds(i * GC, GC)]
            return v.partition_broadcast(P)

        @block.sync
        def _(sp):
            def iteration(phase, i, prev):
                for n, slot, u, j, job, k in iteration_units(phase, i):
                    if k == 0 and bias_of(phase, j):
                        bslot, number = bias_number(phase, i, j)
                        if not (peeled(i) and phase.unit0 == 0):
                            sp.wait_ge(acc_read, job_number(phase, i, j) - 1)
                        sp.dma_start(bias[:, bslot, 0:job.width] if job.width != NCOL or phase.name == "merge" else
                                     bias[:, bslot, :].rearrange("p (g c) -> p g c", g=2),
                                     bias_source(phase, i, j)).then_inc(bias_full[bslot], 16)
                    if not (peeled(i) and phase.unit0 == 0 and u < RING):
                        sp.wait_ge(split_done, n - (RING - 1))
                    src = source(phase, i, j, k)
                    if job.loads == 1:
                        sp.dma_start(w_raw[:, slot, :, 0:job.width], src).then_inc(raw_full[slot], 16)
                    else:
                        for g in range(2):
                            half = src[:, :, g, :] if len(src.shape) == 4 else src[:, :, g * GC:(g + 1) * GC]
                            sp.dma_start(w_raw[:, slot, :, g * GC:(g + 1) * GC], half).then_inc(raw_full[slot], 16)
                    if phase.name == "out" and u == 2 * LEAD:
                        sp.wait_ge(unit_used, PHASE["out"].unit0)
                        sp.dma_start(res[:], x[0].rearrange("(t p) c -> p t c", p=P)).then_inc(res_here, 16)
                        sp.dma_start(g_final[:], norm_final.partition_broadcast(P)).then_inc(final_here, 16)

            run_phases(sp, iteration)
            for n in range(NT):
                for t in range(TT):
                    sp.wait_ge(final_done, n * TT + t + 1)
                    sp.dma_start(out[0, t * P:(t + 1) * P, n * NCOL:(n + 1) * NCOL],
                                 res[:, t, n * NCOL:(n + 1) * NCOL]).then_inc(stored, 16)
            sp.wait_ge(stored, 16 * NT * TT)

        @block.gpsimd
        def _(pool):
            nc.gpsimd.memset(ident[:], 0.0)
            nc.gpsimd.memset(mask_add[:], 0.0)
            nc.gpsimd.memset(mask_mul[:], 1.0)
            nc.gpsimd.memset(minus_one[:], -1.0)
            nc.gpsimd.memset(plus_one[:], 1.0)
            nc.gpsimd.memset(eps[:], EPS)
            nc.gpsimd.memset(buf_b[:, :, 0, GC:GC + 1], 1.0)
            nc.gpsimd.memset(ones_row[:], 1.0).then_inc(pool_order, 1)
            pool.wait_ge(pool_order, 1)
            nc.gpsimd.affine_select(out=ident[:], in_=ident[:], compare_op=ALU.not_equal, fill=1.0, base=0,
                                    pattern=[[-1, P]], channel_multiplier=1)
            for c in (0, 2):
                nc.gpsimd.affine_select(out=mask_add[:, c, :], in_=mask_add[:, c, :], compare_op=ALU.is_ge,
                                        fill=-1e30, base=0, pattern=[[-1, P]], channel_multiplier=1)
            nc.gpsimd.affine_select(out=mask_mul[:], in_=mask_mul[:], compare_op=ALU.is_ge,
                                    fill=0.0, base=0, pattern=[[1, P]], channel_multiplier=-1).then_inc(consts, 1)

        @block.tensor
        def _(pe):
            def turn(dst, src):
                return pe.matmul(dst, src, ident[0:src.shape[0], 0:src.shape[0]], is_transpose=True)

            def start_group(g):
                if g == 0:
                    pe.wait_ge(mem_here, 16)
                if g == KD // 2:
                    pe.wait_ge(x_here, 16)
                if g >= 4:
                    pe.wait_ge(start_lo, g - 3)
                src = mem_in if g < KD // 2 else x_in
                for k in range(2):
                    kt = (2 * g + k) % KD
                    for t in range(TT):
                        last = turn(att[:, g % 4, k * SEQ + t * P:k * SEQ + (t + 1) * P],
                                    src[:, t, kt * P:(kt + 1) * P])
                last.then_inc(start_turned, 1)

            def small_products():
                pe.wait_ge(small_split, 1)
                for t in range(TT):
                    for k in range(KD):
                        for a, b in ((u_hi, small_hi), (u_hi, small_lo), (u_lo, small_hi)):
                            last = pe.matmul(att[:, 3, t * SMALL:(t + 1) * SMALL], a[:, k, t * P:(t + 1) * P],
                                             b[:, k, :], start=(k == 0 and a is u_hi and b is small_hi),
                                             stop=(k == KD - 1 and a is u_lo))
                last.then_inc(small_mm, 1)

            def small_turn():
                pe.wait_ge(small_dve, 2)
                for t in range(TT):
                    turn(att[0:FOX_H, 3, t * P:(t + 1) * P], log_sig[:, t, 0:FOX_H])
                    turn(att[0:ML_H, 3, SEQ + t * P:SEQ + (t + 1) * P], z[:, t, FOX_H:FOX_H + ML_H])
                for t in range(TT):
                    last = turn(att[0:ML_H, 2, t * P:(t + 1) * P], log_sig[:, t, FOX_H + ML_H:SMALL])
                last.then_inc(small_pe, 1)

            def small_back():
                pe.wait_ge(small_dve, 3)
                for t in range(TT):
                    turn(att[:, 3, t * ML_H:(t + 1) * ML_H], a_ml[:, t * P:(t + 1) * P])
                for t in range(TT):
                    last = turn(att[:, 2, t * ML_H:(t + 1) * ML_H], fm_ml[:, t * P:(t + 1) * P])
                last.then_inc(small_pe, 1)

            def mem_turn_qk(a):
                pe.wait_ge(acc_read, a * 2 + (PHASE["mem"].job0 + 2))
                for d in range(2):
                    for t in range(TT):
                        turn(att[:, 0, d * SEQ + t * P:d * SEQ + (t + 1) * P], buf_b[:, t, 0, d * P:(d + 1) * P])
                        last = turn(att[:, 1, d * SEQ + t * P:d * SEQ + (t + 1) * P],
                                    buf_a[:, t, d * P:(d + 1) * P])
                last.then_inc(step_pe["mem"], 1)

            def mem_scores(a):
                pe.wait_ge(step_dve["mem"], a * DVE_STEPS["mem"] + 1)
                pe.wait_ge(step_act["mem"], a * ACT_STEPS["mem"] + 1)
                for t in range(TT):
                    for d in range(2):
                        last = pe.matmul(att[:, 2, t * MEM_LEN:(t + 1) * MEM_LEN],
                                         buf_x[:, d, t * P:(t + 1) * P],
                                         buf_x[:, 2 + d, 0:MEM_LEN], start=(d == 0), stop=(d == 1))
                last.then_inc(step_pe["mem"], 1)

            def mem_turn_p(a):
                pe.wait_ge(step_dve["mem"], a * DVE_STEPS["mem"] + 3)
                for m in range(2):
                    for t in range(TT):
                        last = turn(att[:, 0, m * SEQ + t * P:m * SEQ + (t + 1) * P],
                                    buf_p[:, t, m * P:(m + 1) * P])
                last.then_inc(step_pe["mem"], 1)

            def mem_values(a):
                pe.wait_ge(step_dve["mem"], a * DVE_STEPS["mem"] + 4)
                for e in range(2):
                    for m in range(2):
                        last = pe.matmul(att[:, 1, e * SEQ:(e + 1) * SEQ],
                                         buf_a[:, m, GC + e * P:GC + (e + 1) * P], buf_t[:, m, :],
                                         start=(m == 0), stop=(m == 1))
                last.then_inc(step_pe["mem"], 1)

            def ml_turn_qk(a):
                pe.wait_ge(acc_read, a * 2 + (PHASE["ml"].job0 + 2))
                for g in range(4):
                    for t in range(TT):
                        last = turn(att[:, g // 2, (g % 2) * SEQ + t * P:(g % 2) * SEQ + (t + 1) * P],
                                    buf_a[:, t, g * P:(g + 1) * P])
                last.then_inc(step_pe["ml"], 1)

            def ml_scores(a):
                pe.wait_ge(step_dve["ml"], a * DVE_STEPS["ml"] + 2)
                for s, cols, ts in ((0, slice(0, SEQ), slice(0, SEQ)), (1, slice(SEQ, SEQ + P), slice(P, SEQ))):
                    for d in range(2):
                        pe.matmul(att[:, 2, cols], buf_t[:, 2 + d, s * P:(s + 1) * P], buf_t[:, d, ts],
                                  start=(d == 0), stop=(d == 1))
                last = pe.matmul(att[:, 3, 0:SEQ], plus_one[:], buf_f[0:ML_H, 0, :], start=True, stop=True)
                last.then_inc(step_pe["ml"], 1)

            def ml_values(a):
                pe.wait_ge(step_dve["ml"], a * DVE_STEPS["ml"] + 4)
                p_t = buf_p[:, 2:4, :].rearrange("p a b -> p (a b)")
                pe.matmul(att[:, 0, 0:GC + 1], p_t[:, 0:P], buf_b[:, 0, 0, 0:GC + 1], start=True, stop=True)
                pe.matmul(att[:, 1, 0:GC + 1], p_t[:, P:2 * P], buf_b[:, 0, 0, 0:GC + 1], start=True, stop=False)
                last = pe.matmul(att[:, 1, 0:GC + 1], p_t[:, 2 * P:3 * P], buf_b[:, 1, 0, 0:GC + 1],
                                 start=False, stop=True)
                last.then_inc(step_pe["ml"], 1)

            def ml_turn_y(a):
                pe.wait_ge(step_dve["ml"], a * DVE_STEPS["ml"] + 6)
                for e in range(2):
                    for t in range(TT):
                        last = turn(att[:, 2, e * SEQ + t * P:e * SEQ + (t + 1) * P],
                                    buf_y[:, t, e * P:(e + 1) * P])
                last.then_inc(step_pe["ml"], 1)

            def fox_turn_qk(a):
                pe.wait_ge(acc_read, a * 2 + (PHASE["fox"].job0 + 2))
                for h in range(2):
                    for g in range(2):
                        for t in range(TT):
                            last = turn(att[:, h, g * SEQ + t * P:g * SEQ + (t + 1) * P],
                                        buf_a[:, t, g * GC + h * P:g * GC + (h + 1) * P])
                last.then_inc(step_pe["fox"], 1)

            def fox_scores(a):
                pe.wait_ge(step_dve["fox"], a * DVE_STEPS["fox"] + 2)
                pe.wait_ge(step_act["fox"], a * ACT_STEPS["fox"] + 1)
                for h in range(2):
                    for t, cols, n in ((0, slice(0, P), P), (1, slice(P, P + SEQ), SEQ)):
                        pe.matmul(att[:, 2 + h, cols], buf_x[:, 2 * h, t * P:(t + 1) * P],
                                  buf_x[:, 2 * h + 1, 0:n], start=True, stop=False)
                        last = pe.matmul(att[:, 2 + h, cols], minus_one[:], buf_f[:, h, 0:n],
                                         start=False, stop=True)
                    last.then_inc(step_pe["fox"], 1)

            def fox_turn_p(a):
                pe.wait_ge(step_dve["fox"], a * DVE_STEPS["fox"] + 4)
                for h in range(2):
                    p_h = buf_p[:, 2 * h:2 * h + 2, :].rearrange("p a b -> p (a b)")
                    for c in range(3):
                        last = turn(att[:, h, c * P:(c + 1) * P], p_h[:, c * P:(c + 1) * P])
                last.then_inc(step_pe["fox"], 1)

            def fox_values(a):
                pe.wait_ge(step_dve["fox"], a * DVE_STEPS["fox"] + 5)
                pe.wait_ge(step_act["fox"], a * ACT_STEPS["fox"] + 4)
                for h in range(2):
                    p_t = buf_t[:, 2 * h:2 * h + 2, :].rearrange("p a b -> p (a b)")
                    pe.matmul(att[:, 2, h * SEQ:(h + 1) * SEQ], buf_b[:, 0, 0, h * P:(h + 1) * P],
                              p_t[:, 0:SEQ], start=True, stop=False)
                    last = pe.matmul(att[:, 2, h * SEQ + P:(h + 1) * SEQ], buf_b[:, 1, 0, h * P:(h + 1) * P],
                                     p_t[:, SEQ:SEQ + P], start=False, stop=True)
                last.then_inc(step_pe["fox"], 1)

            def turn_tile(src, q, jobs):
                pe.wait_ge(acc_read, jobs)
                for b in range(2):
                    for k in range(2):
                        for t in range(TT):
                            last = turn(att[:, b, k * SEQ + t * P:k * SEQ + (t + 1) * P],
                                        src[:, t, (2 * b + k) * P:(2 * b + k + 1) * P])
                    last.then_inc(tile_turned, 1)

            def tile_split(q):
                pe.wait_ge(tile_lo, q * 2 + 2)

            def y_split(b):
                def wait(a):
                    pe.wait_ge(y_done[b], a + 1)
                return wait

            ATTENTION = {"mem": {0: mem_turn_qk, 2: mem_scores, 4: mem_turn_p, 6: mem_values, 9: y_split("mem")},
                         "ml": {0: ml_turn_qk, 5: ml_scores, 8: ml_values, 12: ml_turn_y, 15: y_split("ml")},
                         "fox": {0: fox_turn_qk, 3: fox_scores, 7: fox_turn_p, 10: fox_values, 13: y_split("fox")}}

            def after_unit(phase, i, prev, u):
                if prev is None:
                    if 4 + u < KD:
                        start_group(4 + u)
                elif prev.name in ATTENTION:
                    if u in ATTENTION[prev.name]:
                        ATTENTION[prev.name][u](GROUPS - 1 if peeled(i) else i - 1)
                if phase.name == "ml" and prev.name == "mem":
                    for at_unit, do in ((8, small_products), (10, small_turn), (12, small_back)):
                        if u == at_unit:
                            do()
                    if u == 15:
                        pe.wait_ge(small_dve, 4)
                        pe.wait_ge(small_act, 3)
                q = tile_turned_in(phase, i, prev, u, 1)
                if q is not None:
                    turn_tile(*q)
                q = tile_turned_in(phase, i, prev, u, 5)
                if q is not None:
                    tile_split(q[1])

            def tile_turned_in(phase, i, prev, u, place):
                jobs = job_number(phase, i, phase.units[u][0])
                j, k = phase.units[u]
                if k != place:
                    return None
                if phase.name == "merge" and prev is phase and j == 0:
                    return merged, i - 1, jobs
                if phase.name == "out":
                    if j == 0:
                        return merged, NT - 1, jobs
                    return res[:, :, (j - 1) * NCOL:j * NCOL], NT + j - 1, jobs
                if phase.name == "ffn_a" and prev.name == "out" and j == 0:
                    return res[:, :, (NT - 1) * NCOL:NT * NCOL], 2 * NT - 1, jobs
                if phase.name in ("ffn_a", "ffn_b") and prev is phase and j == 0:
                    return buf_a, i + (TILE0[phase.name] - 1), jobs
                if phase.name in ("down_a", "down_b") and j == 0:
                    return buf_a, TILE0["ffn_a"] + (FT_A if phase.name == "down_a" else FT) - 1, jobs
                return None

            def ready_operand(phase, i, prev, j, k):
                if prev is None:
                    pe.wait_ge(start_lo, (KD // UK) * j + k + 1)
                if phase.name == "merge" and prev.name == "fox" and j == 5 and k == 0:
                    pe.wait_ge(y_done["fox"], GROUPS)
                if phase.name == "merge" and prev.name == "fox" and j == 1 and k == 0:
                    pe.wait_ge(y_done["mem"], GROUPS)
                    pe.wait_ge(y_done["ml"], GROUPS)
                per_tile = NCOL // P // UK
                if phase.name == "out" and j == 0 and k in (0, (NT - 1) * per_tile):
                    pe.wait_ge(tile_lo, 2 * (NT - 1 if k == 0 else NT))
                if phase.name == "ffn_a" and prev.name == "out" and j == 0 and k in (0, (NT - 1) * per_tile):
                    pe.wait_ge(tile_lo, 2 * (2 * NT - 1 if k == 0 else 2 * NT))
                if phase.name in ("down_a", "down_b") and j == 0:
                    tiles = phase.jobs[0].kts * P // NCOL
                    done = TILE0["ffn_a"] + (FT_A if phase.name == "down_a" else FT)
                    if k in (0, (tiles - 1) * per_tile):
                        pe.wait_ge(tile_lo, 2 * (done - 1 if k == 0 else done))

            def iteration(phase, i, prev):
                for n, slot, u, j, job, k in iteration_units(phase, i):
                    if k == 0 and prev is not None:
                        pe.wait_ge(acc_read, job_number(phase, i, j) - 1)
                    ready_operand(phase, i, prev, j, k)
                    pe.wait_ge(split_done, n + 1)
                    hi, lo = lhs[job.lhs]
                    for kk in range(UK):
                        kt = k * UK + kk
                        for t in range(TT):
                            for a, b in ((hi, w_hi), (hi, w_lo), (lo, w_hi)):
                                last = pe.matmul(acc[:, 2 * (j % 2) + t, 0:job.width],
                                                 a[:, kt, t * P:(t + 1) * P], b[:, slot, kk, 0:job.width],
                                                 start=(kt == 0 and a is hi and b is w_hi),
                                                 stop=(kt == job.kts - 1 and a is lo))
                    last.then_inc(unit_used, 1)
                    after_unit(phase, i, prev, u)

            pe.wait_ge(consts, 1)
            pe.wait_ge(vecs_in, 96)
            turn(att[:, 3, 0:P], vec_rows[:])
            turn(att[:, 3, P:P + KW], ml_rows[:]).then_inc(vecs_turned, 1)
            for g in range(3):
                start_group(g)
            pe.wait_ge(vecs_done, 1)
            start_group(3)
            run_phases(pe, iteration)

        @block.scalar
        def _(act):
            def round_unit(n, slot, number, width, first):
                act.wait_ge(raw_full[slot], number * 16)
                if not first:
                    act.wait_ge(unit_used, n - (RING - 1))
                act.activation(w_hi[:, slot, :, 0:width], w_raw[:, slot, :, 0:width], ACT.Copy).then_inc(hi_done, 1)

            def start_group(g):
                act.wait_ge(start_turned, g + 1)
                hi = mem_hi if g < KD // 2 else u_hi
                for k in range(2):
                    kt = (2 * g + k) % KD
                    gain = (V_MEM if g < KD // 2 else V_MIX) + kt
                    last = act.activation(hi[:, kt, :], att[:, g % 4, k * SEQ:(k + 1) * SEQ], ACT.Copy,
                                          scale=vec[:, gain:gain + 1])
                last.then_inc(start_hi, 1)

            def square_start(which):
                src = (mem_in, x_in)[which]
                for t in range(TT):
                    if which or t:
                        act.wait_ge(squared, which * TT + t)
                    act.activation(squares[:], src[:, t, :], ACT.Square,
                                   accum_out=ssq[:, which, t, 0:1]).then_inc(squared, 1)

            def root(which):
                act.wait_ge(mean_sq, which + 1)
                act.activation(rstd[:, which, :], rstd[:, which, :], ACT.Sqrt).then_inc(rooted, 1)

            def small_round():
                act.wait_ge(small_here, 32)
                act.activation(small_hi[:], small_raw[:], ACT.Copy).then_inc(small_hi_done, 1)

            def small_log():
                act.wait_ge(small_dve, 1)
                act.activation(z_abs[:], z_abs[:], ACT.Exp, scale=-1.0).then_inc(small_act, 1)
                act.wait_ge(small_act, 1)
                act.activation(z_abs[:], z_abs[:], ACT.Ln, bias=1.0).then_inc(small_act, 1)

            def small_floor():
                act.wait_ge(small_pe, 2)
                act.activation(floor_col[:], att[:, 2, 0:TT * ML_H].rearrange("p (t h) -> p t h", t=TT), ACT.Exp,
                               scale=-1.0).then_inc(small_act, 1)

            def mem_k(a):
                act.wait_ge(step_pe["mem"], a * 4 + 1)
                act.activation(buf_x[:, 2:4, 0:SEQ], att[:, 1, :].rearrange("p (d t) -> p d t", d=2),
                               ACT.Copy).then_inc(step_act["mem"], 1)

            def mem_exp(a):
                act.wait_ge(step_dve["mem"], a * 4 + 2)
                for t in range(TT):
                    act.activation(buf_p[:, t, :], att[:, 2, t * MEM_LEN:(t + 1) * MEM_LEN], ACT.Exp,
                                   bias=stat[:, 0, t:t + 1], accum_out=stat[:, 1, t:t + 1]
                                   ).then_inc(step_act["mem"], 1)

            def mem_y(a):
                act.wait_ge(step_pe["mem"], a * 4 + 4)
                act.activation(y["mem"][0][:, bass.ds(a * 2, 2), :], att[:, 1, :].rearrange("p (e t) -> p e t", e=2),
                               ACT.Copy).then_inc(y_hi["mem"], 1)

            def ml_pad(a):
                act.wait_ge(step_pe["ml"], a * 4 + 1)
                for b in range(2):
                    act.activation(buf_x[:, 2 * b:2 * b + 2, 3:3 + SEQ],
                                   att[:, b, :].rearrange("p (d t) -> p d t", d=2), ACT.Copy
                                   ).then_inc(step_act["ml"], 1)

            def ml_sigmoids(a):
                act.wait_ge(step_dve["ml"], a * 6 + 1)
                act.activation(buf_t[:], buf_p[:], ACT.Sigmoid).then_inc(step_act["ml"], 1)
                act.activation(buf_b[:, :, 1, 0:GC], buf_b[:, :, 1, 0:GC], ACT.Sigmoid)

            def ml_exp(a):
                act.wait_ge(step_dve["ml"], a * 6 + 3)
                act.activation(buf_p[:, 0:2, :].rearrange("p a b -> p (a b)")[:, 0:3 * P],
                               buf_p[:, 0:2, :].rearrange("p a b -> p (a b)")[:, 0:3 * P], ACT.Exp,
                               scale=-1.0).then_inc(step_act["ml"], 1)

            def ml_square(a):
                act.wait_ge(step_dve["ml"], a * 6 + 5)
                for t in range(TT):
                    act.activation(buf_t[:, t, :], att[:, t, 0:GC], ACT.Square, scale=stat[:, 2, t:t + 1],
                                   accum_out=stat[:, 1, t:t + 1]).then_inc(step_act["ml"], 1)
                act.wait_ge(step_act["ml"], a * 7 + 6)
                act.activation(stat[:, 3, 0:2], stat[:, 1, 0:2], ACT.Sqrt, scale=1.0 / ML_D,
                               bias=eps[:, 0:1]).then_inc(step_act["ml"], 1)

            def ml_y(a):
                act.wait_ge(step_pe["ml"], a * 4 + 4)
                for e in range(2):
                    last = act.activation(y["ml"][0][:, bass.ds(a * 2 + e, 1), :].rearrange("p a t -> p (a t)"),
                                          att[:, 2, e * SEQ:(e + 1) * SEQ],
                                          ACT.Copy, scale=ml_gain[:, bass.ds(a * 2 + e, 1)])
                last.then_inc(y_hi["ml"], 1)

            def fox_qk(a):
                act.wait_ge(step_pe["fox"], a * 5 + 1)
                act.activation(buf_x[:, 2, 0:SEQ], att[:, 1, 0:SEQ], ACT.Copy, scale=FOX_D ** -0.5)
                act.activation(buf_x[:, 3, 0:SEQ], att[:, 1, SEQ:2 * SEQ], ACT.Copy).then_inc(step_act["fox"], 1)

            def fox_exp(a):
                act.wait_ge(step_dve["fox"], a * 5 + 3)
                for h in range(2):
                    p_h = buf_p[:, 2 * h:2 * h + 2, :].rearrange("p a b -> p (a b)")
                    for t, cols in ((0, slice(0, P)), (1, slice(P, 3 * P))):
                        c = 2 * h + t
                        last = act.activation(p_h[:, cols], p_h[:, cols], ACT.Exp, bias=stat[:, 0, c:c + 1],
                                              accum_out=stat[:, 1, c:c + 1])
                    last.then_inc(step_act["fox"], 1)

            def fox_p(a):
                act.wait_ge(step_pe["fox"], a * 5 + 4)
                act.activation(buf_t[:, 2:4, :].rearrange("p a b -> p (a b)")[:, 0:3 * P], att[:, 1, 0:3 * P],
                               ACT.Copy).then_inc(step_act["fox"], 1)

            def fox_y(a):
                act.wait_ge(step_pe["fox"], a * 5 + 5)
                act.activation(y["fox"][0][:, bass.ds(a * 2, 2), :], att[:, 2, :].rearrange("p (e t) -> p e t", e=2),
                               ACT.Copy).then_inc(y_hi["fox"], 1)

            def tile_hi_part(dst, kt0, q, gain=None):
                for b in range(2):
                    act.wait_ge(tile_turned, q * 2 + b + 1)
                    if gain is None:
                        last = act.activation(dst[:, bass.ds(kt0 + 2 * b, 2), :],
                                              att[:, b, :].rearrange("p (k t) -> p k t", k=2), ACT.Copy)
                    else:
                        for k in range(2):
                            kt = kt0 + 2 * b + k
                            last = act.activation(dst[:, kt, :], att[:, b, k * SEQ:(k + 1) * SEQ], ACT.Copy,
                                                  scale=vec[:, gain + kt:gain + kt + 1])
                    last.then_inc(tile_hi, 1)

            def square_tile(which, n, ready):
                act.wait_ge(ready[0], ready[1])
                for t in range(TT):
                    act.activation(scratch[:], res[:, t, n * NCOL:(n + 1) * NCOL], ACT.Square,
                                   accum_out=ssq[:, which, t, n:n + 1]).then_inc(squared, 1)
                    if not (n == NT - 1 and t == TT - 1 and which == 3):
                        act.wait_ge(squared, (which * TT if which < 2 else 2 * TT + (which - 2) * TT * NT) + n * TT + t + 1)

            ATTENTION = {"mem": {0: mem_k, 2: mem_exp, 6: mem_y},
                         "ml": {0: ml_pad, 2: ml_sigmoids, 5: ml_exp, 9: ml_square, 12: ml_y},
                         "fox": {0: fox_qk, 3: fox_exp, 7: fox_p, 10: fox_y}}

            def after_unit(phase, i, prev, u, n):
                last_of_job = u + 1 == len(phase.units) or phase.units[u + 1][1] == 0
                if prev is None:
                    if 4 + u < KD:
                        start_group(4 + u)
                    if u == 5:
                        square_start(0)
                    if u == 6:
                        root(0)
                    if u == 12:
                        square_start(1)
                    if u == 13:
                        root(1)
                elif prev.name in ATTENTION:
                    if u in ATTENTION[prev.name]:
                        ATTENTION[prev.name][u](GROUPS - 1 if peeled(i) else i - 1)
                if phase.name == "ml" and prev.name == "mem":
                    for at_unit, do in ((6, small_round), (9, small_log), (12, small_floor)):
                        if u == at_unit:
                            do()
                if phase.name == "merge":
                    if u == 1 and prev.name == "merge":
                        tile_hi_part(merged_hi, (i - 1) * 4, i - 1)
                    if last_of_job and phase.units[u][0] % 2 == 0:
                        j = phase.units[u][0] // 2
                        act.wait_ge(acc_read, job_number(phase, i, 2 * j) + 1)
                        act.activation(gate[:], gate[:], ACT.Sigmoid).then_inc(gate_done, 1)
                if phase.name == "out":
                    j = u // (KD // UK)
                    if u % (KD // UK) == 1:
                        if j == 0:
                            tile_hi_part(merged_hi, (NT - 1) * 4, NT - 1)
                        else:
                            tile_hi_part(u_hi, (j - 1) * 4, NT + j - 1, V_FFN)
                    if last_of_job:
                        square_tile(2, j, (acc_read, job_number(phase, i, j) + 1))
                if phase.name in ("ffn_a", "ffn_b"):
                    if u == 1:
                        if prev.name == "out":
                            tile_hi_part(u_hi, (NT - 1) * 4, 2 * NT - 1, V_FFN)
                        elif prev is phase:
                            tile_hi_part(h_hi, (i - 1) * 4, i + (TILE0[phase.name] - 1))
                    if prev.name == "out" and u == 3:
                        root(2)
                    if last_of_job and phase.units[u][0] == 0:
                        act.wait_ge(unit_used, n + 1)
                        act.wait_ge(rstd_done, 3)
                        for t in range(TT):
                            act.activation(gate[:, t, :], acc[:, t, :], ACT.Sigmoid,
                                           scale=rstd[:, 2, t:t + 1]).then_inc(ffn_sig, 1)
                if phase.name in ("down_a", "down_b"):
                    if u == 1:
                        tiles = FT_A if phase.name == "down_a" else FT - FT_A
                        q = TILE0["ffn_a"] + (FT_A if phase.name == "down_a" else FT) - 1
                        tile_hi_part(h_hi, (tiles - 1) * 4, q)
                    if last_of_job and phase.name == "down_b":
                        j = phase.units[u][0]
                        square_tile(3, j, (acc_read, job_number(phase, i, j) + 1))

            def loads_of_slot(phase, i, u):
                s, per = u % RING, len(phase.units)
                if u >= per and phase.iters == 1:
                    following = PHASES[PHASES.index(phase) + 1]
                    return following.loads0[s] + following.jobs[0].loads
                before = phase.loads0[s] + phase.per_slot[s] * (u // per)
                return i * phase.per_slot[s] + (before + sum(phase.jobs[j].loads for j, _ in
                                                             phase.units[s:u % per + 1:RING]))

            def ahead(phase, i, u):
                m = u + LEAD
                per = len(phase.units)
                if m < per:
                    width = phase.jobs[phase.units[m][0]].width
                else:
                    if phase is PHASES[-1] and m >= per:
                        return
                    width = NCOL
                round_unit(i * per + (phase.unit0 + m), m % RING, loads_of_slot(phase, i, m), width,
                           phase.unit0 == 0 and peeled(i) and m < RING)

            def iteration(phase, i, prev):
                for n, slot, u, j, job, k in iteration_units(phase, i):
                    ahead(phase, i, u)
                    after_unit(phase, i, prev, u, n)

            act.dma_start(mem_in[:], mem[0].rearrange("(t p) c -> p t c", p=P)).then_inc(mem_here, 16)
            rows = lambda v: v.rearrange("(r c) -> r c", c=P)
            act.dma_start(ml_rows[:], rows(mlstm_norm[0])).then_inc(vecs_in, 16)
            for r0, v in ((V_MIX, norm_mix[0]), (V_MEM, norm_mem[0]), (V_FFN, norm_ffn[0]), (V_CB, conv_b[0])):
                act.dma_start(vec_rows[r0:r0 + KD, :], rows(v)).then_inc(vecs_in, 16)
            act.dma_start(vec_rows[V_CW:V_CW + 4 * KD, :],
                          conv_w[0].rearrange("j (r c) -> (j r) c", c=P)).then_inc(vecs_in, 16)
            act.dma_start(x_in[:], x[0].rearrange("(t p) c -> p t c", p=P)).then_inc(x_here, 16)
            small_w = w_in[0].rearrange("(k p) c -> p k c", p=P)
            act.dma_start(small_raw[:, :, 0:FOX_H], small_w[:, :, FOX_F:FOX_F + FOX_H]).then_inc(small_here, 16)
            act.dma_start(small_raw[:, :, FOX_H:SMALL], small_w[:, :, ML_I:ML_I + 2 * ML_H]).then_inc(small_here, 16)
            act.dma_start(small_bias[:, 0:FOX_H], b_in[0, FOX_F:FOX_F + FOX_H].partition_broadcast(P)
                          ).then_inc(small_bias_here, 16)
            act.dma_start(small_bias[:, FOX_H:SMALL], b_in[0, ML_I:ML_I + 2 * ML_H].partition_broadcast(P)
                          ).then_inc(small_bias_here, 16)
            for u in range(LEAD):
                round_unit(u, u, PHASES[0].jobs[0].loads, NCOL, True)
            act.wait_ge(vecs_done, 1)
            for g in range(4):
                start_group(g)
            run_phases(act, iteration)
            root(3)

        @block.vector
        def _(dve):
            chain = Chain(dve, dve_order, LINKS)
            link = chain.link

            def split_unit(n, slot, width):
                dve.wait_ge(hi_done, n + 1)
                dve.tensor_tensor(w_lo[:, slot, :, 0:width], w_raw[:, slot, :, 0:width],
                                  w_hi[:, slot, :, 0:width].bitcast(F32), ALU.subtract).then_inc(split_done, 1)

            def start_group(g):
                dve.wait_ge(start_hi, g + 1)
                hi, lo = (mem_hi, mem_lo) if g < KD // 2 else (u_hi, u_lo)
                for k in range(2):
                    kt = (2 * g + k) % KD
                    gain = (V_MEM if g < KD // 2 else V_MIX) + kt
                    last = dve.scalar_tensor_tensor(lo[:, kt, :], att[:, g % 4, k * SEQ:(k + 1) * SEQ],
                                                    vec[:, gain:gain + 1], hi[:, kt, :].bitcast(F32),
                                                    ALU.mult, ALU.subtract)
                last.then_inc(start_lo, 1)

            def mean_square(which, count, tiles):
                dve.wait_ge(squared, count)
                if tiles == 1:
                    dve.tensor_scalar(rstd[:, which, :], ssq[:, which, :, 0], 1.0 / D, EPS, ALU.mult, ALU.add
                                      ).then_inc(mean_sq, 1)
                else:
                    link(dve.tensor_reduce(rstd[:, which, :], ssq[:, which, :, :], AX_X, ALU.add))
                    dve.tensor_scalar(rstd[:, which, :], rstd[:, which, :], 1.0 / D, EPS, ALU.mult, ALU.add
                                      ).then_inc(mean_sq, 1)

            def invert(which):
                dve.wait_ge(rooted, which + 1)
                dve.reciprocal(rstd[:, which, :], rstd[:, which, :]).then_inc(rstd_done, 1)
                dve.wait_ge(rstd_done, which + 1)

            def small_remainder():
                dve.wait_ge(small_hi_done, 1)
                dve.tensor_tensor(small_lo[:], small_raw[:], small_hi[:].bitcast(F32), ALU.subtract
                                  ).then_inc(small_split, 1)

            def small_logits():
                dve.wait_ge(small_mm, 1)
                dve.wait_ge(small_bias_here, 32)
                for t in range(TT):
                    last = dve.scalar_tensor_tensor(z[:, t, :], att[:, 3, t * SMALL:(t + 1) * SMALL],
                                                    rstd[:, 1, t:t + 1], small_bias[:], ALU.mult, ALU.add)
                link(last)
                dve.scalar_tensor_tensor(z_abs[:], z[:], -1.0, z[:], ALU.mult, ALU.max).then_inc(small_dve, 1)

            def small_log_sigmoid():
                dve.wait_ge(small_act, 2)
                dve.scalar_tensor_tensor(log_sig[:], z[:], 0.0, z_abs[:], ALU.min, ALU.subtract
                                         ).then_inc(small_dve, 1)

            def small_scans():
                dve.wait_ge(small_pe, 1)
                dve.tensor_tensor_scan(f_fox[:], ones_row[:], att[0:FOX_H, 3, 0:SEQ], 0.0, ALU.mult, ALU.add)
                link(dve.tensor_tensor_scan(f_ml[:], ones_row[0:ML_H, :], att[0:ML_H, 2, 0:SEQ], 0.0,
                                            ALU.mult, ALU.add))
                link(dve.tensor_tensor(a_ml[:], att[0:ML_H, 3, SEQ:2 * SEQ], f_ml[:], ALU.subtract))
                link(dve.tensor_tensor_scan(m_ml[:], ones_row[0:ML_H, :], a_ml[:], 0.0, ALU.mult, ALU.max))
                dve.tensor_tensor(fm_ml[:], f_ml[:], m_ml[:], ALU.add).then_inc(small_dve, 1)

            def small_columns():
                dve.wait_ge(small_pe, 2)
                dve.tensor_copy(a_col[:], att[:, 3, 0:TT * ML_H].rearrange("p (t h) -> p t h", t=TT)
                                ).then_inc(small_dve, 1)

            def y_lo(b, a):
                dve.wait_ge(y_hi[b], a + 1)
                bank = 1 if b == "mem" else 2
                dve.tensor_tensor(y[b][1][:, bass.ds(a * 2, 2), :], att[:, bank, :].rearrange("p (e t) -> p e t", e=2),
                                  y[b][0][:, bass.ds(a * 2, 2), :].bitcast(F32), ALU.subtract
                                  ).then_inc(y_done[b], 1)

            def mem_q(a):
                dve.wait_ge(step_pe["mem"], a * 4 + 1)
                dve.tensor_scalar(buf_x[:, 0:2, 0:SEQ], att[:, 0, :].rearrange("p (d t) -> p d t", d=2),
                                  MEM_D ** -0.5, None, ALU.mult).then_inc(step_dve["mem"], 1)

            def mem_max(a):
                dve.wait_ge(step_pe["mem"], a * 4 + 2)
                link(dve.tensor_reduce(stat[:, 2, 0:2], att[:, 2, :].rearrange("p (t m) -> p t m", t=TT), AX_X,
                                       ALU.max))
                dve.tensor_scalar(stat[:, 0, 0:2], stat[:, 2, 0:2], -1.0, None, ALU.mult
                                  ).then_inc(step_dve["mem"], 1)
                dve.wait_ge(step_act["mem"], a * 3 + 3)
                link(dve.reciprocal(stat[:, 2, 0:2], stat[:, 1, 0:2]))
                for t in range(TT):
                    last = dve.tensor_scalar(buf_p[:, t, :], buf_p[:, t, :], stat[:, 2, t:t + 1], None, ALU.mult)
                last.then_inc(step_dve["mem"], 1)

            def mem_p(a):
                dve.wait_ge(step_pe["mem"], a * 4 + 3)
                dve.tensor_copy(buf_t[:, 0:2, :], att[:, 0, :].rearrange("p (m t) -> p m t", m=2)
                                ).then_inc(step_dve["mem"], 1)

            def mem_y(a):
                y_lo("mem", a)

            def conv_tap(a, tap):
                for g in range(4):
                    c = (g // 2) * KW + g % 2
                    w_tap = vec[:, bass.ds(a * 2 + (V_CW + tap * KD + c), 1)]
                    if tap == 3:
                        last = dve.tensor_scalar(buf_p[:, g, :], buf_x[:, g, tap:tap + SEQ], w_tap,
                                                 vec[:, bass.ds(a * 2 + (V_CB + c), 1)], ALU.mult, ALU.add)
                    else:
                        last = dve.scalar_tensor_tensor(buf_p[:, g, :], buf_x[:, g, tap:tap + SEQ], w_tap,
                                                        buf_p[:, g, :], ALU.mult, ALU.add)
                return last

            def ml_conv_1(a):
                dve.wait_ge(step_act["ml"], a * 7 + 2)
                link(conv_tap(a, 3))
                link(conv_tap(a, 2))

            def ml_conv_2(a):
                link(conv_tap(a, 1))
                conv_tap(a, 0).then_inc(step_dve["ml"], 1)

            def ml_silu(a):
                dve.tensor_scalar(buf_f[0:ML_H, 0, :], m_ml[:], ident[0:ML_H, bass.ds(a, 1)], None, ALU.mult)
                dve.wait_ge(step_act["ml"], a * 7 + 3)
                dve.tensor_tensor(buf_t[:, 0:2, :], buf_p[:, 0:2, :], buf_t[:, 0:2, :], ALU.mult)
                dve.scalar_tensor_tensor(buf_t[:, 2:4, :], buf_p[:, 2:4, :], ML_D ** -0.5, buf_t[:, 2:4, :],
                                         ALU.mult, ALU.mult).then_inc(step_dve["ml"], 1)

            def ml_weights(a):
                dve.wait_ge(step_pe["ml"], a * 4 + 2)
                e = buf_p[:, 0:2, :].rearrange("p a b -> p (a b)")
                dve.tensor_scalar(e[:, 0:SEQ], att[:, 3, 0:SEQ], a_col[:, 0, bass.ds(a, 1)], 0.0,
                                  ALU.subtract, ALU.max)
                dve.tensor_scalar(e[:, SEQ:SEQ + P], att[:, 3, P:SEQ], a_col[:, 1, bass.ds(a, 1)], 0.0,
                                  ALU.subtract, ALU.max).then_inc(step_dve["ml"], 1)
                dve.wait_ge(step_act["ml"], a * 7 + 4)
                dve.tensor_tensor(e[:, 0:P], e[:, 0:P], mask_mul[:], ALU.mult)
                link(dve.tensor_tensor(e[:, SEQ:SEQ + P], e[:, SEQ:SEQ + P], mask_mul[:], ALU.mult))
                p_t = buf_p[:, 2:4, :].rearrange("p a b -> p (a b)")
                dve.tensor_tensor(p_t[:, 0:3 * P], att[:, 2, 0:3 * P], e[:, 0:3 * P], ALU.mult
                                  ).then_inc(step_dve["ml"], 1)

            def ml_denominator(a):
                dve.wait_ge(step_pe["ml"], a * 4 + 3)
                for t in range(TT):
                    last = dve.tensor_scalar(stat[:, 0, t:t + 1], att[:, t, GC:GC + 1],
                                             floor_col[:, t, bass.ds(a, 1)], None, ALU.max)
                link(last)
                for t in range(TT):
                    last = dve.scalar_tensor_tensor(stat[:, 0, t:t + 1], att[:, t, GC:GC + 1], -1.0,
                                                    stat[:, 0, t:t + 1], ALU.mult, ALU.max)
                link(last)
                dve.reciprocal(stat[:, 2, 0:2], stat[:, 0, 0:2]).then_inc(step_dve["ml"], 1)

            def ml_output(a):
                dve.wait_ge(step_act["ml"], a * 7 + 7)
                link(dve.reciprocal(stat[:, 0, 0:2], stat[:, 3, 0:2]))
                link(dve.tensor_tensor(stat[:, 0, 2:4], stat[:, 0, 0:2], stat[:, 2, 0:2], ALU.mult))
                for t in range(TT):
                    last = dve.scalar_tensor_tensor(buf_y[:, t, :], att[:, t, 0:GC], stat[:, 0, 2 + t:3 + t],
                                                    buf_b[:, t, 1, 0:GC], ALU.mult, ALU.mult)
                last.then_inc(step_dve["ml"], 1)

            def ml_y(a):
                dve.wait_ge(y_hi["ml"], a + 1)
                for e in range(2):
                    last = dve.scalar_tensor_tensor(
                        y["ml"][1][:, bass.ds(a * 2 + e, 1), :].rearrange("p a t -> p (a t)"),
                        att[:, 2, e * SEQ:(e + 1) * SEQ], ml_gain[:, bass.ds(a * 2 + e, 1)],
                        y["ml"][0][:, bass.ds(a * 2 + e, 1), :].rearrange("p a t -> p (a t)").bitcast(F32),
                        ALU.mult, ALU.subtract)
                last.then_inc(y_done["ml"], 1)

            def fox_qk(a):
                for h in range(2):
                    last = dve.tensor_scalar(buf_f[:, h, :], f_fox[:], ident[0:FOX_H, bass.ds(a * 2 + h, 1)], None,
                                             ALU.mult)
                last.then_inc(step_dve["fox"], 1)
                dve.wait_ge(step_pe["fox"], a * 5 + 1)
                dve.tensor_scalar(buf_x[:, 0, 0:SEQ], att[:, 0, 0:SEQ], FOX_D ** -0.5, None, ALU.mult)
                dve.tensor_copy(buf_x[:, 1, 0:SEQ], att[:, 0, SEQ:2 * SEQ]).then_inc(step_dve["fox"], 1)

            def fox_max(a):
                for h in range(2):
                    dve.wait_ge(step_pe["fox"], a * 5 + 2 + h)
                    p_h = buf_p[:, 2 * h:2 * h + 2, :].rearrange("p a b -> p (a b)")
                    link(dve.tensor_tensor(p_h[:, 0:3 * P], att[:, 2 + h, 0:3 * P],
                                           mask_add[:].rearrange("p a b -> p (a b)"), ALU.add))
                    dve.tensor_reduce(stat[:, 2, 2 * h:2 * h + 1], p_h[:, 0:P], AX_X, ALU.max)
                    last = dve.tensor_reduce(stat[:, 2, 2 * h + 1:2 * h + 2], p_h[:, P:3 * P], AX_X, ALU.max)
                    link(last)
                dve.tensor_scalar(stat[:, 0, :], stat[:, 2, :], -1.0, None, ALU.mult
                                  ).then_inc(step_dve["fox"], 1)
                dve.wait_ge(step_act["fox"], a * 4 + 3)
                link(dve.reciprocal(stat[:, 2, :], stat[:, 1, :]))
                for h in range(2):
                    p_h = buf_p[:, 2 * h:2 * h + 2, :].rearrange("p a b -> p (a b)")
                    for t, cols in ((0, slice(0, P)), (1, slice(P, 3 * P))):
                        c = 2 * h + t
                        last = dve.tensor_scalar(p_h[:, cols], p_h[:, cols], stat[:, 2, c:c + 1], None, ALU.mult)
                last.then_inc(step_dve["fox"], 1)

            def fox_p(a):
                dve.wait_ge(step_pe["fox"], a * 5 + 4)
                dve.tensor_copy(buf_t[:, 0:2, :].rearrange("p a b -> p (a b)")[:, 0:3 * P], att[:, 0, 0:3 * P]
                                ).then_inc(step_dve["fox"], 1)

            def fox_y(a):
                y_lo("fox", a)

            def tile_lo_part(hi, lo, kt0, q, gain=None):
                for b in range(2):
                    dve.wait_ge(tile_hi, q * 2 + b + 1)
                    if gain is None:
                        last = dve.tensor_tensor(lo[:, bass.ds(kt0 + 2 * b, 2), :],
                                                 att[:, b, :].rearrange("p (k t) -> p k t", k=2),
                                                 hi[:, bass.ds(kt0 + 2 * b, 2), :].bitcast(F32), ALU.subtract)
                    else:
                        for k in range(2):
                            kt = kt0 + 2 * b + k
                            last = dve.scalar_tensor_tensor(lo[:, kt, :], att[:, b, k * SEQ:(k + 1) * SEQ],
                                                            vec[:, gain + kt:gain + kt + 1],
                                                            hi[:, kt, :].bitcast(F32), ALU.mult, ALU.subtract)
                    last.then_inc(tile_lo, 1)

            ATTENTION = {"mem": {0: mem_q, 2: mem_max, 4: mem_p, 6: mem_y},
                         "ml": {0: ml_conv_1, 1: ml_conv_2, 3: ml_silu, 5: ml_weights, 8: ml_denominator,
                                9: ml_output, 12: ml_y},
                         "fox": {0: fox_qk, 3: fox_max, 7: fox_p, 10: fox_y}}

            def finish_job(phase, i, prev, j, n):
                job = phase.jobs[j]
                bank = 2 * (j % 2)
                number = job_number(phase, i, j)
                dve.wait_ge(unit_used, n + 1)
                if not (peeled(i) and phase.job0 == 0 and j == 0):
                    dve.wait_ge(acc_read, number)
                b = bias_of(phase, j)
                if b:
                    slot, load = bias_number(phase, i, j)
                    dve.wait_ge(bias_full[slot], load * 16 + 16)
                if phase.name in ATTENTION:
                    if prev is not None:
                        a = GROUPS - 1 if peeled(i) else i - 1
                        steps = {"mem": (4, 1), "ml": (1, 3), "fox": (1, 5)}[prev.name][j]
                        dve.wait_ge(step_pe[prev.name], a * PE_STEPS[prev.name] + steps)
                    for t in range(TT):
                        src = acc[:, bank + t, 0:job.width]
                        dst = buf_a[:, t, :] if j == 0 else buf_b[:, t, 0, 0:GC]
                        bb = bias[:, b[0], 0:job.width] if b else None
                        if phase.name == "ml" and j == 1:
                            dst = buf_b[:, t, :, 0:GC]
                            src = src.rearrange("p (g c) -> p g c", g=2)
                            bb = bb.rearrange("p (g c) -> p g c", g=2)
                        if b:
                            last = dve.scalar_tensor_tensor(dst, src, rstd[:, 1, t:t + 1], bb, ALU.mult, ALU.add)
                        else:
                            last = dve.tensor_scalar(dst, src, rstd[:, 0, t:t + 1], None, ALU.mult)
                elif phase.name == "merge" and j % 2 == 0:
                    for t in range(TT):
                        last = dve.scalar_tensor_tensor(gate[:, t, :], acc[:, bank + t, :], rstd[:, 1, t:t + 1],
                                                        bias[:, b[0], :], ALU.mult, ALU.add)
                elif phase.name == "merge":
                    dve.wait_ge(gate_done, i * 3 + (j // 2 + 1))
                    if j == 1 and not peeled(i):
                        dve.wait_ge(tile_turned, i * 2)
                    for t in range(TT):
                        if j == 1:
                            last = dve.tensor_tensor(merged[:, t, :], acc[:, bank + t, :], gate[:, t, :], ALU.mult)
                        else:
                            link(dve.tensor_tensor(scratch[:], acc[:, bank + t, :], gate[:, t, :], ALU.mult))
                            last = dve.tensor_tensor(merged[:, t, :], merged[:, t, :], scratch[:], ALU.add)
                            if t + 1 < TT:
                                link(last)
                elif phase.name in ("out", "down_a", "down_b"):
                    if phase.name == "out" and j == 0:
                        dve.wait_ge(res_here, 16)
                    cols = slice(j * NCOL, (j + 1) * NCOL)
                    for t in range(TT):
                        last = dve.tensor_tensor(res[:, t, cols], acc[:, bank + t, :], res[:, t, cols], ALU.add)
                elif j == 0:
                    tiles = 0 if phase.name == "ffn_a" else FT_A
                    for t in range(TT):
                        dve.wait_ge(ffn_sig, i * TT + (tiles * TT + t + 1))
                        last = dve.scalar_tensor_tensor(merged[:, t, :], acc[:, bank + t, :], rstd[:, 2, t:t + 1],
                                                        gate[:, t, :], ALU.mult, ALU.mult)
                else:
                    dve.wait_ge(tile_turned, i * 2 + 2 * TILE0[phase.name])
                    for t in range(TT):
                        last = dve.scalar_tensor_tensor(buf_a[:, t, :], acc[:, bank + t, :], rstd[:, 2, t:t + 1],
                                                        merged[:, t, :], ALU.mult, ALU.mult)
                last.then_inc(acc_read, 1)

            def after_unit(phase, i, prev, u, n):
                if prev is None and u == 7:
                    invert(0)
                if prev is None and u == 15:
                    invert(1)
                if u + 1 == len(phase.units) or phase.units[u + 1][1] == 0:
                    finish_job(phase, i, prev, phase.units[u][0], n)
                if prev is None:
                    if 4 + u < KD:
                        start_group(4 + u)
                    if u == 6:
                        mean_square(0, TT, 1)
                    if u == 13:
                        mean_square(1, 2 * TT, 1)
                elif prev.name in ATTENTION and u in ATTENTION[prev.name]:
                    ATTENTION[prev.name][u](GROUPS - 1 if peeled(i) else i - 1)
                if phase.name == "ml" and prev.name == "mem":
                    for at_unit, do in ((7, small_remainder), (9, small_logits), (10, small_log_sigmoid),
                                        (11, small_scans), (12, small_columns)):
                        if u == at_unit:
                            do()
                    if u == 12:
                        dve.memset(buf_x[:, :, 0:3], 0.0)
                if phase.name == "merge" and prev is phase and u == 1:
                    tile_lo_part(merged_hi, merged_lo, (i - 1) * 4, i - 1)
                if phase.name == "out" and u % (KD // UK) == 1:
                    j = u // (KD // UK)
                    if j == 0:
                        tile_lo_part(merged_hi, merged_lo, (NT - 1) * 4, NT - 1)
                    else:
                        tile_lo_part(u_hi, u_lo, (j - 1) * 4, NT + j - 1, V_FFN)
                if phase.name in ("ffn_a", "ffn_b") and u == 1:
                    if prev.name == "out":
                        tile_lo_part(u_hi, u_lo, (NT - 1) * 4, 2 * NT - 1, V_FFN)
                        mean_square(2, 2 * TT + TT * NT, NT)
                    elif prev is phase:
                        tile_lo_part(h_hi, h_lo, (i - 1) * 4, i + (TILE0[phase.name] - 1))
                if phase.name == "ffn_a" and prev.name == "out" and u == 4:
                    invert(2)
                if phase.name in ("down_a", "down_b") and u == 1:
                    tiles = FT_A if phase.name == "down_a" else FT - FT_A
                    q = TILE0["ffn_a"] + (FT_A if phase.name == "down_a" else FT) - 1
                    tile_lo_part(h_hi, h_lo, (tiles - 1) * 4, q)

            def ahead(phase, i, u):
                m = u + LEAD
                per = len(phase.units)
                if m >= per and phase is PHASES[-1]:
                    return
                width = phase.jobs[phase.units[m][0]].width if m < per else NCOL
                split_unit(i * per + (phase.unit0 + m), m % RING, width)

            def iteration(phase, i, prev):
                for n, slot, u, j, job, k in iteration_units(phase, i):
                    ahead(phase, i, u)
                    after_unit(phase, i, prev, u, n)

            dve.wait_ge(vecs_turned, 1)
            dve.tensor_copy(vec[:], att[:, 3, 0:P])
            dve.tensor_copy(ml_gain[:], att[:, 3, P:P + KW]).then_inc(vecs_done, 1)
            dve.wait_ge(vecs_done, 1)
            for u in range(LEAD):
                split_unit(u, u, NCOL)
            for g in range(4):
                start_group(g)
            run_phases(dve, iteration, chain)
            mean_square(3, 2 * TT + 2 * TT * NT, NT)
            invert(3)
            dve.wait_ge(final_here, 16)
            for n in range(NT):
                cols = slice(n * NCOL, (n + 1) * NCOL)
                for t in range(TT):
                    dve.scalar_tensor_tensor(res[:, t, cols], res[:, t, cols], rstd[:, 3, t:t + 1],
                                             g_final[:, cols], ALU.mult, ALU.mult).then_inc(final_done, 1)


def kernel(x, mem, norm_mix, w_in, b_in, conv_w, conv_b, mlstm_norm, norm_mem, w_mem_kv, w_br_fox,
           w_br_mlstm, w_br_mem, w_out, norm_ffn, w_ffn_in, w_ffn_out, norm_final):
    import numpy as np
    import concourse.bacc as bacc
    from concourse import mybir as mb
    from concourse.bass_utils import run_bass_kernel_spmd

    given = dict(x=x, mem=mem, norm_mix=norm_mix, w_in=w_in, b_in=b_in, conv_w=conv_w, conv_b=conv_b,
                 mlstm_norm=mlstm_norm, norm_mem=norm_mem, w_mem_kv=w_mem_kv, w_br_fox=w_br_fox,
                 w_br_mlstm=w_br_mlstm, w_br_mem=w_br_mem, w_out=w_out, norm_ffn=norm_ffn,
                 w_ffn_in=w_ffn_in, w_ffn_out=w_ffn_out, norm_final=norm_final)
    nc = bacc.Bacc("TRN2", target_bir_lowering=False, num_devices=1)
    arrays, args = {}, {}
    for name, value in given.items():
        a = np.ascontiguousarray(value)
        arrays["in_" + name] = a
        args[name] = nc.dram_tensor("in_" + name, a.shape, mb.dt.from_np(a.dtype), kind="ExternalInput").ap()
    out = nc.dram_tensor("out_y", (1, SEQ, D), mb.dt.float32, kind="ExternalOutput").ap()
    hybrid_layer(nc, out=out, **args)
    return run_bass_kernel_spmd(nc, [arrays], core_ids=[0]).results[0]["out_y"]
```

```python
from contextlib import ExitStack

import concourse.bass as bass
from concourse import mybir

F32 = mybir.dt.float32
F32R = mybir.dt.float32r
ALU = mybir.AluOpType
ACT = mybir.ActivationFunctionType
AX_X = mybir.AxisListType.X

P = 128
SEQ = 256
TT = SEQ // P
D = 2048
KD = D // P
NCOL = 512
UK = 2
NT = D // NCOL
EPS = 1e-6
MEM_LEN = 256
FOX_H, FOX_D = 8, 128
ML_H, ML_D = 4, 256
MEM_D = 256
W = 1024
KW = W // P
D_FF = -(-8 * D // (3 * 256)) * 256
FT = D_FF // NCOL
FT_A = (FT + 1) // 2
RING = 4
LEAD = RING - 1
EARLY = 2
GROUPS = 4
GC = W // GROUPS

FOX_Q, FOX_F = 0, 3 * W
ML_Q = FOX_F + FOX_H
ML_V = ML_Q + 2 * W
ML_I = ML_Q + 3 * W
ML_O = ML_I + 2 * ML_H
MEM_Q = ML_O + W
GATES = MEM_Q + W
SMALL = FOX_H + 2 * ML_H


class Job:

    def __init__(self, lhs, kts, width, loads=1):
        self.lhs, self.kts, self.width, self.loads = lhs, kts, width, loads
        self.units = kts // UK


class Phase:
    def __init__(self, name, jobs, iters):
        self.name, self.jobs, self.iters = name, jobs, iters
        self.units = [(j, k) for j, job in enumerate(jobs) for k in range(job.units)]


def phases():
    out = [
        Phase("mem", [Job("mem", KD, NCOL, 2), Job("u", KD, GC)], GROUPS),
        Phase("ml", [Job("u", KD, NCOL, 2), Job("u", KD, NCOL, 2)], GROUPS),
        Phase("fox", [Job("u", KD, NCOL, 2), Job("u", KD, GC)], GROUPS),
        Phase("merge", [Job("u", KD, NCOL, 2), Job("y_mem", KW, NCOL), Job("u", KD, NCOL),
                        Job("y_ml", KW, NCOL), Job("u", KD, NCOL), Job("y_fox", KW, NCOL)], NT),
        Phase("out", [Job("merged", KD, NCOL, 2)] + [Job("merged", KD, NCOL)] * (NT - 1), 1),
        Phase("ffn_a", [Job("u", KD, NCOL), Job("u", KD, NCOL)], FT_A),
        Phase("down_a", [Job("hidden", FT_A * NCOL // P, NCOL)] * NT, 1),
        Phase("ffn_b", [Job("u", KD, NCOL), Job("u", KD, NCOL)], FT - FT_A),
        Phase("down_b", [Job("hidden", (FT - FT_A) * NCOL // P, NCOL)] * NT, 1),
    ]
    unit = job = 0
    loads = [0] * RING
    for p in out:
        p.unit0, p.job0, p.loads0 = unit, job, list(loads)
        p.per_slot = [sum(p.jobs[j].loads for j, _ in p.units[s::RING]) for s in range(RING)]
        loads = [a + b * p.iters for a, b in zip(loads, p.per_slot)]
        unit += len(p.units) * p.iters
        job += len(p.jobs) * p.iters
        assert len(p.units) % RING == 0 and len(p.jobs) % 2 == 0
    for p, q in zip(out, out[1:]):
        assert p.iters == 1 or p.jobs[0].loads == q.jobs[0].loads
    return out


PHASES = phases()
PHASE = {p.name: p for p in PHASES}

LINKS = {"mem": 2, "ml": 8, "fox": 5, "merge": 6, "ffn_a": 0, "ffn_b": 0}


class Chain:

    def __init__(self, engine, sem, links):
        self.engine, self.sem, self.links, self.n, self.turn = engine, sem, links, 0, None

    def link(self, instruction):
        instruction.then_inc(self.sem, 1)
        self.n += 1
        value = self.n if self.turn is None else self.turn + self.n
        self.engine.wait_ge(self.sem, value)

    def enter(self, i, first, phase):
        self.per = self.links[phase]
        self.turn, self.at = (i - first) * self.per, self.n

    def leave(self, turns):
        assert self.n - self.at == self.per, (self.n - self.at, self.per)
        self.n, self.turn = self.at + self.per * turns, None


def peeled(i):
    return isinstance(i, int)


def run_phases(engine, iteration, chain=None):
    for prev, phase in zip([None] + PHASES, PHASES):
        iteration(phase, 0, prev)
        if phase.iters > 1:
            with engine.Fori(1, phase.iters) as i:
                if chain:
                    chain.enter(i, 1, phase.name)
                iteration(phase, i, phase)
            if chain:
                chain.leave(phase.iters - 1)


def hybrid_layer(nc, x, mem, norm_mix, w_in, b_in, conv_w, conv_b, mlstm_norm, norm_mem, w_mem_kv,
                 w_br_fox, w_br_mlstm, w_br_mem, w_out, norm_ffn, w_ffn_in, w_ffn_out, norm_final, out):
    ctx = ExitStack()
    place = [(nc.sbuf_base + 63) // 64 * 64]

    def at(name, shape, dt, offset):
        return nc.alloc_sbuf_tensor_at(name, shape, dt, offset=offset)

    def sb(name, shape, dt=F32):
        size = 4
        for s in shape[1:]:
            size *= s
        offset = place[0]
        place[0] += (size + 31) // 32 * 32
        assert place[0] <= nc.sbuf_top, (name, place[0])
        return at(name, shape, dt, offset)

    with ctx:
        def sem(name):
            return ctx.enter_context(nc.semaphore(name))

        w_raw = sb("w_raw", [P, RING, UK, NCOL])
        w_hi = sb("w_hi", [P, RING, UK, NCOL], F32R)
        w_lo = sb("w_lo", [P, RING, UK, NCOL], F32R)
        bias = sb("bias", [P, 2, NCOL])

        u_hi = sb("u_hi", [P, KD, SEQ], F32R)
        u_lo = sb("u_lo", [P, KD, SEQ], F32R)
        region_b = place[0]
        mem_hi = sb("mem_hi", [P, KD, SEQ], F32R)
        mem_lo = sb("mem_lo", [P, KD, SEQ], F32R)
        region_c = place[0]
        y = {}
        for b in ("mem", "ml", "fox"):
            y[b] = (sb(f"y_{b}_hi", [P, KW, SEQ], F32R), sb(f"y_{b}_lo", [P, KW, SEQ], F32R))
        operand = KD * SEQ * 4
        rows = TT * D * 4
        hidden = FT_A * NCOL // P * SEQ * 4
        merged_hi = at("merged_hi", [P, KD, SEQ], F32R, region_b)
        merged_lo = at("merged_lo", [P, KD, SEQ], F32R, region_b + operand)
        squares = at("squares", [P, TT * NT, NCOL], F32, region_c)
        mem_in = at("mem_in", [P, TT, D], F32, region_c + rows)
        x_in = at("x_in", [P, TT, D], F32, region_c + 2 * rows)
        res = at("res", [P, TT, D], F32, region_c)
        h_hi = at("h_hi", [P, FT_A * NCOL // P, SEQ], F32R, region_c + rows)
        h_lo = at("h_lo", [P, FT_A * NCOL // P, SEQ], F32R, region_b)
        g_final = at("g_final", [P, D], F32, region_c + rows + hidden)
        lhs = {"mem": (mem_hi, mem_lo), "u": (u_hi, u_lo), "merged": (merged_hi, merged_lo),
               "hidden": (h_hi, h_lo), "y_mem": y["mem"], "y_ml": y["ml"], "y_fox": y["fox"]}

        buf_a = sb("buf_a", [P, TT, NCOL])
        buf_b = sb("buf_b", [P, TT, 2, GC + 4])
        buf_x = sb("buf_x", [P, 4, SEQ + 4])
        buf_p = sb("buf_p", [P, 4, SEQ])
        buf_t = sb("buf_t", [P, 4, SEQ])
        buf_y = sb("buf_y", [P, TT, GC])
        buf_f = sb("buf_f", [FOX_H, 2, SEQ])
        region_g = place[0]
        gate = sb("gate", [P, TT, NCOL])
        region_m = place[0]
        merged = sb("merged", [P, TT, NCOL])
        scratch = sb("scratch", [P, NCOL])

        small, row = KD * SMALL * 4, SEQ * 4
        small_raw = at("small_raw", [P, KD, SMALL], F32, region_g)
        small_hi = at("small_hi", [P, KD, SMALL], F32R, region_g + small)
        small_lo = at("small_lo", [P, KD, SMALL], F32R, region_g + 2 * small)
        small_rows = at("small_rows", [SMALL, SEQ], F32, region_g + 3 * small)
        ones_row = at("ones_row", [FOX_H, SEQ], F32, region_m)
        f_ml = at("f_ml", [ML_H, SEQ], F32, region_m + row)
        a_ml = at("a_ml", [ML_H, SEQ], F32, region_m + 2 * row)
        fm_ml = at("fm_ml", [ML_H, SEQ], F32, region_m + 3 * row)
        f_fox = sb("f_fox", [FOX_H, SEQ])
        m_ml = sb("m_ml", [ML_H, SEQ])
        small_bias = sb("small_bias", [P, SMALL])
        z = sb("z", [P, TT, SMALL])
        z_abs = sb("z_abs", [P, TT, SMALL])
        log_sig = sb("log_sig", [P, TT, SMALL])
        a_col = sb("a_col", [P, TT, ML_H])
        floor_col = sb("floor_col", [P, TT, ML_H])

        ident = sb("ident", [P, P])
        mask_add = sb("mask_add", [P, 3, P])
        mask_mul = sb("mask_mul", [P, P])
        minus_one = sb("minus_one", [FOX_H, P])
        plus_one = sb("plus_one", [ML_H, P])
        eps = sb("eps", [P, 1])
        vec_rows = sb("vec_rows", [7 * KD, P])
        vec = sb("vec", [P, 8 * KD])
        mem_gain_rows = sb("mem_gain_rows", [KD, P])
        ml_rows = sb("ml_rows", [KW, P])
        ml_gain = sb("ml_gain", [P, KW])
        V_MIX, V_FFN, V_CB, V_CW = 0, KD, 2 * KD, 3 * KD
        VR = V_CW + 4 * KD
        V_MEM = VR
        ssq = sb("ssq", [P, 4, TT, NT])
        rstd = sb("rstd", [P, 4, TT])
        warm = sb("warm", [P, 2])
        stat = sb("stat", [P, 4, 4])

        acc = ctx.enter_context(nc.psum_tensor("acc", [P, 4, NCOL], F32))
        att = ctx.enter_context(nc.psum_tensor("att", [P, 4, NCOL], F32))

        raw_full = [sem(f"raw_full{s}") for s in range(RING)]
        hi_done, split_done, unit_used = sem("hi_done"), sem("split_done"), sem("unit_used")
        acc_read = sem("acc_read")
        bias_full = [sem("bias_full0"), sem("bias_full1")]
        eps_set, ident_set, consts = sem("eps_set"), sem("ident_set"), sem("consts")
        mem_gain_in, vecs_in, vecs_turned, vecs_done = (
            sem("mem_gain_in"), sem("vecs_in"), sem("vecs_turned"), sem("vecs_done"))
        mem_first = sem("mem_first")
        mem_here, x_here = [[sem(f"{v}_here{c}") for c in range(NT)] for v in ("mem", "x")]
        small_here, small_bias_here, res_here, final_here = (
            sem("small_here"), sem("small_bias_here"), sem("res_here"), sem("final_here"))
        start_turned, start_hi, start_lo = sem("start_turned"), sem("start_hi"), sem("start_lo")
        squared, mean_sq, rooted, rstd_done = sem("squared"), sem("mean_sq"), sem("rooted"), sem("rstd_done")
        small_hi_done, small_split, small_act, small_dve, small_pe = (
            sem("small_hi_done"), sem("small_split"), sem("small_act"), sem("small_dve"),
            sem("small_pe"))
        step_pe = {b: sem(f"{b}_step_pe") for b in ("mem", "ml", "fox")}
        step_dve = {b: sem(f"{b}_step_dve") for b in ("mem", "ml", "fox")}
        step_act = {b: sem(f"{b}_step_act") for b in ("mem", "ml", "fox")}
        y_hi = {b: sem(f"{b}_y_hi") for b in ("mem", "ml", "fox")}
        y_done = {b: sem(f"{b}_y_done") for b in ("mem", "ml", "fox")}
        gate_done = sem("gate_done")
        tile_turned, tile_hi, tile_lo = sem("tile_turned"), sem("tile_hi"), sem("tile_lo")
        ffn_sig, stored = sem("ffn_sig"), sem("stored")
        last_sums, last_res, gained, final_dve, final_act = (
            sem("last_sums"), sem("last_res"), sem("gained"), sem("final_dve"), sem("final_act"))
        dve_order, pool_order = sem("dve_order"), sem("pool_order")
        block = ctx.enter_context(nc.Block())

        PE_STEPS = {"mem": 4, "ml": 4, "fox": 5}
        DVE_STEPS = {"mem": 4, "ml": 6, "fox": 5}
        ACT_STEPS = {"mem": 3, "ml": 7, "fox": 4}

        def pe_steps(branch, a, k):
            return a * PE_STEPS[branch] + k

        def dve_steps(branch, a, k):
            return a * DVE_STEPS[branch] + k

        def act_steps(branch, a, k):
            return a * ACT_STEPS[branch] + k

        TILE0 = {"merge": 0, "out": NT, "ffn_a": 2 * NT, "ffn_b": 2 * NT + FT_A}

        def iteration_units(phase, i):
            for u, (j, k) in enumerate(phase.units):
                yield i * len(phase.units) + (phase.unit0 + u), u % RING, u, j, phase.jobs[j], k

        def job_number(phase, i, j):
            return i * len(phase.jobs) + (phase.job0 + j)

        def pair(w, first, step, i, rows):
            v = w[:, first:first + 2 * step].rearrange("(k p) (g c) -> p k g c", p=P, g=2)
            return v[:, rows, :, bass.ds(i * GC, GC)]

        def flat(w, cols, rows):
            return w.rearrange("(k p) c -> p k c", p=P)[:, rows, cols]

        def source(phase, i, j, k):
            rows = slice(k * UK, (k + 1) * UK)
            if phase.name == "mem":
                return pair(w_mem_kv[0], 0, W, i, rows) if j == 0 else \
                    flat(w_in[0], bass.ds(i * GC + MEM_Q, GC), rows)
            if phase.name == "ml":
                return pair(w_in[0], ML_Q, W, i, rows) if j == 0 else pair(w_in[0], ML_V, ML_O - ML_V, i, rows)
            if phase.name == "fox":
                return pair(w_in[0], FOX_Q, W, i, rows) if j == 0 else \
                    flat(w_in[0], bass.ds(i * GC + 2 * W, GC), rows)
            if phase.name == "merge":
                b = 2 - j // 2
                if j % 2 == 0:
                    return flat(w_in[0], bass.ds(i * NCOL + (GATES + b * D), NCOL), rows)
                return flat((w_br_fox, w_br_mlstm, w_br_mem)[b][0], bass.ds((i - 1) * NCOL + NCOL, NCOL), rows)
            if phase.name == "out":
                return flat(w_out[0], slice(j * NCOL, (j + 1) * NCOL), rows)
            tile0 = 0 if phase.name.endswith("a") else FT_A
            if phase.name.startswith("ffn"):
                return flat(w_ffn_in[0], bass.ds(i * NCOL + (tile0 * NCOL + j * D_FF), NCOL), rows)
            kt0 = tile0 * NCOL // P
            rows = slice(kt0 + k * UK, kt0 + (k + 1) * UK)
            return flat(w_ffn_out[0], slice(j * NCOL, (j + 1) * NCOL), rows)

        def bias_of(phase, j):
            if phase.name == "mem":
                return (1, 0, 1) if j == 1 else None
            if phase.name in ("ml", "fox"):
                return (j, 0, 1)
            if phase.name == "merge" and j % 2 == 0:
                return ((j // 2) % 2, j // 4, 2 - (j // 2) % 2)
            return None

        BIAS0 = {"mem": (0, 0), "ml": (0, GROUPS), "fox": (GROUPS, 2 * GROUPS), "merge": (2 * GROUPS, 3 * GROUPS)}

        def bias_number(phase, i, j):
            slot, k, per = bias_of(phase, j)
            return slot, i * per + (BIAS0[phase.name][slot] + k)

        def bias_source(phase, i, j):
            b = b_in[0]
            if phase.name == "mem":
                v = b[bass.ds(i * GC + MEM_Q, GC)]
            elif phase.name == "merge":
                v = b[bass.ds(i * NCOL + (GATES + (2 - j // 2) * D), NCOL)]
            elif phase.name == "fox" and j == 1:
                v = b[bass.ds(i * GC + 2 * W, GC)]
            else:
                first, step = ((FOX_Q, W) if phase.name == "fox" else (ML_Q, W) if j == 0 else (ML_V, ML_O - ML_V))
                v = b[first:first + 2 * step].rearrange("(g c) -> g c", g=2)[:, bass.ds(i * GC, GC)]
            return v.partition_broadcast(P)

        @block.sync
        def _(sp):
            def load_tokens(src, dst, c, here):
                cols = slice(c * NCOL, (c + 1) * NCOL)
                sp.dma_start(dst[:, :, cols], src[0].rearrange("(t p) c -> p t c", p=P)[:, :, cols]
                             ).then_inc(here[c], 16)

            def load_first_tokens(half, here):
                cols = slice(half * GC, (half + 1) * GC)
                sp.dma_start(mem_in[:, :, cols], mem[0].rearrange("(t p) c -> p t c", p=P)[:, :, cols]
                             ).then_inc(here, 16)

            def iteration(phase, i, prev):
                for n, slot, u, j, job, k in iteration_units(phase, i):
                    if k == 0 and bias_of(phase, j):
                        bslot, number = bias_number(phase, i, j)
                        if not (peeled(i) and phase.unit0 == 0):
                            sp.wait_ge(acc_read, job_number(phase, i, j) - 1)
                        sp.dma_start(bias[:, bslot, 0:job.width] if job.width != NCOL or phase.name == "merge" else
                                     bias[:, bslot, :].rearrange("p (g c) -> p g c", g=2),
                                     bias_source(phase, i, j)).then_inc(bias_full[bslot], 16)
                    if not (peeled(i) and phase.unit0 == 0 and u < RING):
                        sp.wait_ge(split_done, n - (RING - 1))
                    if phase.unit0 == 0 and peeled(i):
                        if u == 1:
                            load_first_tokens(1, mem_here[0])
                        if u in (2, 3, 4):
                            load_tokens(mem, mem_in, u - 1, mem_here)
                        elif 5 <= u < 5 + NT:
                            load_tokens(x, x_in, u - 5, x_here)
                        load_rest(u)
                    src = source(phase, i, j, k)
                    if job.loads == 1:
                        sp.dma_start(w_raw[:, slot, :, 0:job.width], src).then_inc(raw_full[slot], 16)
                    else:
                        for g in range(2):
                            half = src[:, :, g, :] if len(src.shape) == 4 else src[:, :, g * GC:(g + 1) * GC]
                            sp.dma_start(w_raw[:, slot, :, g * GC:(g + 1) * GC], half).then_inc(raw_full[slot], 16)
                    if phase.name == "out" and u == 2 * LEAD:
                        sp.wait_ge(unit_used, PHASE["out"].unit0)
                        sp.dma_start(res[:], x[0].rearrange("(t p) c -> p t c", p=P)).then_inc(res_here, 16)
                        sp.dma_start(g_final[:], norm_final.partition_broadcast(P)).then_inc(final_here, 16)

            def load_rest(u):
                def rows(v):
                    return v.rearrange("(r c) -> r c", c=P)
                if u == 2:
                    for r0, v in ((V_MIX, norm_mix[0]), (V_FFN, norm_ffn[0]), (V_CB, conv_b[0])):
                        sp.dma_start(vec_rows[r0:r0 + KD, :], rows(v)).then_inc(vecs_in, 16)
                if u == 3:
                    sp.dma_start(vec_rows[V_CW:V_CW + 4 * KD, :],
                                 conv_w[0].rearrange("j (r c) -> (j r) c", c=P)).then_inc(vecs_in, 16)
                    sp.dma_start(ml_rows[:], rows(mlstm_norm[0])).then_inc(vecs_in, 16)
                for half, cols, first in ((0, slice(0, FOX_H), FOX_F), (1, slice(FOX_H, SMALL), ML_I)):
                    size = cols.stop - cols.start
                    if u == 9 + half:
                        sp.dma_start(small_raw[:, :, cols], w_in[0].rearrange("(k p) c -> p k c", p=P)
                                     [:, :, first:first + size]).then_inc(small_here, 16)
                    if u == 11 + half:
                        sp.dma_start(small_bias[:, cols], b_in[0, first:first + size].partition_broadcast(P)
                                     ).then_inc(small_bias_here, 16)

            sp.dma_start(mem_gain_rows[:], norm_mem[0].rearrange("(r c) -> r c", c=P)).then_inc(mem_gain_in, 16)
            load_first_tokens(0, mem_first)
            run_phases(sp, iteration)
            for t in range(TT):
                for count, (norm_done, n) in enumerate(((final_dve, 0), (final_act, 1), (final_dve, NT - 1),
                                                        (final_act, 2))):
                    sp.wait_ge(norm_done, t * 2 + count // 2 + 1)
                    sp.dma_start(out[0, t * P:(t + 1) * P, n * NCOL:(n + 1) * NCOL],
                                 res[:, t, n * NCOL:(n + 1) * NCOL]).then_inc(stored, 16)
            sp.wait_ge(stored, 16 * NT * TT)

        @block.gpsimd
        def _(pool):
            nc.gpsimd.memset(eps[:], EPS).then_inc(eps_set, 1)
            nc.gpsimd.memset(ident[:], 0.0).then_inc(pool_order, 1)
            pool.wait_ge(pool_order, 1)
            nc.gpsimd.affine_select(out=ident[:], in_=ident[:], compare_op=ALU.not_equal, fill=1.0, base=0,
                                    pattern=[[-1, P]], channel_multiplier=1).then_inc(ident_set, 1)
            nc.gpsimd.memset(mask_add[:], 0.0)
            nc.gpsimd.memset(mask_mul[:], 1.0)
            nc.gpsimd.memset(minus_one[:], -1.0)
            nc.gpsimd.memset(plus_one[:], 1.0)
            nc.gpsimd.memset(buf_b[:, :, 0, GC:GC + 1], 1.0)
            nc.gpsimd.memset(ones_row[:], 1.0).then_inc(pool_order, 1)
            pool.wait_ge(pool_order, 2)
            for c in (0, 2):
                nc.gpsimd.affine_select(out=mask_add[:, c, :], in_=mask_add[:, c, :], compare_op=ALU.is_ge,
                                        fill=-1e30, base=0, pattern=[[-1, P]], channel_multiplier=1)
            nc.gpsimd.affine_select(out=mask_mul[:], in_=mask_mul[:], compare_op=ALU.is_ge,
                                    fill=0.0, base=0, pattern=[[1, P]], channel_multiplier=-1).then_inc(consts, 1)

        @block.tensor
        def _(pe):
            def turn(dst, src):
                return pe.matmul(dst, src, ident[0:src.shape[0], 0:src.shape[0]], is_transpose=True)

            def start_group(g):
                if g == 0:
                    pe.wait_ge(mem_first, 16)
                elif g == 1 or g % 2 == 0:
                    pe.wait_ge((mem_here if g < KD // 2 else x_here)[g % (KD // 2) // 2], 16)
                if g >= 3:
                    pe.wait_ge(start_lo, g - 2)
                src = mem_in if g < KD // 2 else x_in
                for k in range(2):
                    kt = (2 * g + k) % KD
                    for t in range(TT):
                        last = turn(att[:, g % 3, k * SEQ + t * P:k * SEQ + (t + 1) * P],
                                    src[:, t, kt * P:(kt + 1) * P])
                last.then_inc(start_turned, 1)

            def turn_vectors():
                pe.wait_ge(vecs_in, 80)
                pe.wait_ge(vecs_done, 1)
                turn(att[:, 3, 0:VR], vec_rows[:])
                turn(att[:, 3, VR:VR + KW], ml_rows[:]).then_inc(vecs_turned, 1)

            def small_products():
                pe.wait_ge(small_split, 1)
                for k in range(KD):
                    for a, b in ((u_hi, small_hi), (u_hi, small_lo), (u_lo, small_hi)):
                        last = pe.matmul(att[0:SMALL, 3, 0:SEQ], b[:, k, :], a[:, k, :],
                                         start=(k == 0 and a is u_hi and b is small_hi),
                                         stop=(k == KD - 1 and a is u_lo))
                last.then_inc(small_pe, 1)

            def small_tokens():
                pe.wait_ge(small_dve, 1)
                for t in range(TT):
                    last = turn(att[:, 3, t * SMALL:(t + 1) * SMALL], small_rows[:, t * P:(t + 1) * P])
                last.then_inc(small_pe, 1)

            def small_turn():
                pe.wait_ge(small_dve, 3)
                for t in range(TT):
                    turn(att[0:FOX_H, 3, t * P:(t + 1) * P], log_sig[:, t, 0:FOX_H])
                    turn(att[0:ML_H, 3, SEQ + t * P:SEQ + (t + 1) * P], z[:, t, FOX_H:FOX_H + ML_H])
                for t in range(TT):
                    last = turn(att[0:ML_H, 2, t * P:(t + 1) * P], log_sig[:, t, FOX_H + ML_H:SMALL])
                last.then_inc(small_pe, 1)

            def small_back():
                pe.wait_ge(small_dve, 4)
                for t in range(TT):
                    turn(att[:, 3, t * ML_H:(t + 1) * ML_H], a_ml[:, t * P:(t + 1) * P])
                for t in range(TT):
                    last = turn(att[:, 2, t * ML_H:(t + 1) * ML_H], fm_ml[:, t * P:(t + 1) * P])
                last.then_inc(small_pe, 1)

            def mem_turn_qk(a):
                pe.wait_ge(acc_read, a * 2 + (PHASE["mem"].job0 + 2))
                for d in range(2):
                    for t in range(TT):
                        turn(att[:, 0, d * SEQ + t * P:d * SEQ + (t + 1) * P], buf_b[:, t, 0, d * P:(d + 1) * P])
                        last = turn(att[:, 1, d * SEQ + t * P:d * SEQ + (t + 1) * P],
                                    buf_a[:, t, d * P:(d + 1) * P])
                last.then_inc(step_pe["mem"], 1)

            def mem_scores(a):
                pe.wait_ge(step_dve["mem"], dve_steps("mem", a, 1))
                pe.wait_ge(step_act["mem"], act_steps("mem", a, 1))
                for t in range(TT):
                    for d in range(2):
                        last = pe.matmul(att[:, 2, t * MEM_LEN:(t + 1) * MEM_LEN],
                                         buf_x[:, d, t * P:(t + 1) * P],
                                         buf_x[:, 2 + d, 0:MEM_LEN], start=(d == 0), stop=(d == 1))
                last.then_inc(step_pe["mem"], 1)

            def mem_turn_p(a):
                pe.wait_ge(step_dve["mem"], dve_steps("mem", a, 3))
                for m in range(2):
                    for t in range(TT):
                        last = turn(att[:, 0, m * SEQ + t * P:m * SEQ + (t + 1) * P],
                                    buf_p[:, t, m * P:(m + 1) * P])
                last.then_inc(step_pe["mem"], 1)

            def mem_values(a):
                pe.wait_ge(step_dve["mem"], dve_steps("mem", a, 4))
                for e in range(2):
                    for m in range(2):
                        last = pe.matmul(att[:, 1, e * SEQ:(e + 1) * SEQ],
                                         buf_a[:, m, GC + e * P:GC + (e + 1) * P], buf_t[:, m, :],
                                         start=(m == 0), stop=(m == 1))
                last.then_inc(step_pe["mem"], 1)

            def ml_turn_qk(a):
                pe.wait_ge(acc_read, a * 2 + (PHASE["ml"].job0 + 2))
                for g in range(4):
                    for t in range(TT):
                        last = turn(att[:, g // 2, (g % 2) * SEQ + t * P:(g % 2) * SEQ + (t + 1) * P],
                                    buf_a[:, t, g * P:(g + 1) * P])
                last.then_inc(step_pe["ml"], 1)

            def ml_scores(a):
                pe.wait_ge(small_dve, 5)
                pe.wait_ge(small_act, 3)
                pe.wait_ge(step_dve["ml"], dve_steps("ml", a, 2))
                for s, cols, ts in ((0, slice(0, SEQ), slice(0, SEQ)), (1, slice(SEQ, SEQ + P), slice(P, SEQ))):
                    for d in range(2):
                        pe.matmul(att[:, 2, cols], buf_t[:, 2 + d, s * P:(s + 1) * P], buf_t[:, d, ts],
                                  start=(d == 0), stop=(d == 1))
                last = pe.matmul(att[:, 3, 0:SEQ], plus_one[:], buf_f[0:ML_H, 0, :], start=True, stop=True)
                last.then_inc(step_pe["ml"], 1)

            def ml_values(a):
                pe.wait_ge(step_dve["ml"], dve_steps("ml", a, 4))
                p_t = buf_p[:, 2:4, :].rearrange("p a b -> p (a b)")
                pe.matmul(att[:, 0, 0:GC + 1], p_t[:, 0:P], buf_b[:, 0, 0, 0:GC + 1], start=True, stop=True)
                pe.matmul(att[:, 1, 0:GC + 1], p_t[:, P:2 * P], buf_b[:, 0, 0, 0:GC + 1], start=True, stop=False)
                last = pe.matmul(att[:, 1, 0:GC + 1], p_t[:, 2 * P:3 * P], buf_b[:, 1, 0, 0:GC + 1],
                                 start=False, stop=True)
                last.then_inc(step_pe["ml"], 1)

            def ml_turn_y(a):
                pe.wait_ge(step_dve["ml"], dve_steps("ml", a, 6))
                for e in range(2):
                    for t in range(TT):
                        last = turn(att[:, 2, e * SEQ + t * P:e * SEQ + (t + 1) * P],
                                    buf_y[:, t, e * P:(e + 1) * P])
                last.then_inc(step_pe["ml"], 1)

            def fox_turn_qk(a):
                pe.wait_ge(acc_read, a * 2 + (PHASE["fox"].job0 + 2))
                for h in range(2):
                    for g in range(2):
                        for t in range(TT):
                            last = turn(att[:, h, g * SEQ + t * P:g * SEQ + (t + 1) * P],
                                        buf_a[:, t, g * GC + h * P:g * GC + (h + 1) * P])
                last.then_inc(step_pe["fox"], 1)

            def fox_scores(a):
                pe.wait_ge(step_dve["fox"], dve_steps("fox", a, 2))
                pe.wait_ge(step_act["fox"], act_steps("fox", a, 1))
                for h in range(2):
                    for t, cols, n in ((0, slice(0, P), P), (1, slice(P, P + SEQ), SEQ)):
                        pe.matmul(att[:, 2 + h, cols], buf_x[:, 2 * h, t * P:(t + 1) * P],
                                  buf_x[:, 2 * h + 1, 0:n], start=True, stop=False)
                        last = pe.matmul(att[:, 2 + h, cols], minus_one[:], buf_f[:, h, 0:n],
                                         start=False, stop=True)
                    last.then_inc(step_pe["fox"], 1)

            def fox_turn_p(a):
                pe.wait_ge(step_dve["fox"], dve_steps("fox", a, 4))
                for h in range(2):
                    p_h = buf_p[:, 2 * h:2 * h + 2, :].rearrange("p a b -> p (a b)")
                    for c in range(3):
                        last = turn(att[:, h, c * P:(c + 1) * P], p_h[:, c * P:(c + 1) * P])
                last.then_inc(step_pe["fox"], 1)

            def fox_values(a):
                pe.wait_ge(step_dve["fox"], dve_steps("fox", a, 5))
                pe.wait_ge(step_act["fox"], act_steps("fox", a, 4))
                for h in range(2):
                    p_t = buf_t[:, 2 * h:2 * h + 2, :].rearrange("p a b -> p (a b)")
                    pe.matmul(att[:, 2, h * SEQ:(h + 1) * SEQ], buf_b[:, 0, 0, h * P:(h + 1) * P],
                              p_t[:, 0:SEQ], start=True, stop=False)
                    last = pe.matmul(att[:, 2, h * SEQ + P:(h + 1) * SEQ], buf_b[:, 1, 0, h * P:(h + 1) * P],
                                     p_t[:, SEQ:SEQ + P], start=False, stop=True)
                last.then_inc(step_pe["fox"], 1)

            def turn_tile(src, q, jobs):
                pe.wait_ge(acc_read, jobs)
                for b in range(2):
                    for k in range(2):
                        for t in range(TT):
                            last = turn(att[:, b, k * SEQ + t * P:k * SEQ + (t + 1) * P],
                                        src[:, t, (2 * b + k) * P:(2 * b + k + 1) * P])
                    last.then_inc(tile_turned, 1)

            def tile_split(q):
                pe.wait_ge(tile_lo, q * 2 + 2)

            def y_split(b):
                def wait(a):
                    pe.wait_ge(y_done[b], a + 1)
                return wait

            ATTENTION = {"mem": {0: mem_turn_qk, 2: mem_scores, 4: mem_turn_p, 6: mem_values, 9: y_split("mem")},
                         "ml": {0: ml_turn_qk, 6: ml_scores, 9: ml_values, 13: ml_turn_y, 15: y_split("ml")},
                         "fox": {0: fox_turn_qk, 3: fox_scores, 7: fox_turn_p, 10: fox_values, 13: y_split("fox")}}

            def after_unit(phase, i, prev, u):
                if prev is None:
                    if EARLY + u < KD:
                        start_group(EARLY + u)
                    if u == 3:
                        turn_vectors()
                elif prev.name in ATTENTION:
                    if u in ATTENTION[prev.name]:
                        ATTENTION[prev.name][u](GROUPS - 1 if peeled(i) else i - 1)
                if phase.name == "ml" and prev.name == "mem":
                    for at_unit, do in ((1, small_products), (3, small_tokens), (8, small_turn), (11, small_back)):
                        if u == at_unit:
                            do()
                q = tile_turned_in(phase, i, prev, u, 1)
                if q is not None:
                    turn_tile(*q)
                q = tile_turned_in(phase, i, prev, u, 5)
                if q is not None:
                    tile_split(q[1])

            def tile_turned_in(phase, i, prev, u, place):
                jobs = job_number(phase, i, phase.units[u][0])
                j, k = phase.units[u]
                if k != place:
                    return None
                if phase.name == "merge" and prev is phase and j == 0:
                    return merged, i - 1, jobs
                if phase.name == "out":
                    if j == 0:
                        return merged, NT - 1, jobs
                    return res[:, :, (j - 1) * NCOL:j * NCOL], NT + j - 1, jobs
                if phase.name == "ffn_a" and prev.name == "out" and j == 0:
                    return res[:, :, (NT - 1) * NCOL:NT * NCOL], 2 * NT - 1, jobs
                if phase.name in ("ffn_a", "ffn_b") and prev is phase and j == 0:
                    return buf_a, i + (TILE0[phase.name] - 1), jobs
                if phase.name in ("down_a", "down_b") and j == 0:
                    return buf_a, TILE0["ffn_a"] + (FT_A if phase.name == "down_a" else FT) - 1, jobs
                return None

            def ready_operand(phase, i, prev, j, k):
                if prev is None:
                    pe.wait_ge(start_lo, (KD // UK) * j + k + 1)
                if phase.name == "merge" and prev.name == "fox" and j == 5 and k == 0:
                    pe.wait_ge(y_done["fox"], GROUPS)
                if phase.name == "merge" and prev.name == "fox" and j == 1 and k == 0:
                    pe.wait_ge(y_done["mem"], GROUPS)
                    pe.wait_ge(y_done["ml"], GROUPS)
                per_tile = NCOL // P // UK
                if phase.name == "out" and j == 0 and k in (0, (NT - 1) * per_tile):
                    pe.wait_ge(tile_lo, 2 * (NT - 1 if k == 0 else NT))
                if phase.name == "ffn_a" and prev.name == "out" and j == 0 and k in (0, (NT - 1) * per_tile):
                    pe.wait_ge(tile_lo, 2 * (2 * NT - 1 if k == 0 else 2 * NT))
                if phase.name in ("down_a", "down_b") and j == 0:
                    tiles = phase.jobs[0].kts * P // NCOL
                    done = TILE0["ffn_a"] + (FT_A if phase.name == "down_a" else FT)
                    if k in (0, (tiles - 1) * per_tile):
                        pe.wait_ge(tile_lo, 2 * (done - 1 if k == 0 else done))

            def products(slot, j, job, k, token_tiles):
                hi, lo = lhs[job.lhs]
                for kk in range(UK):
                    kt = k * UK + kk
                    for t in token_tiles:
                        for a, b in ((hi, w_hi), (hi, w_lo), (lo, w_hi)):
                            last = pe.matmul(acc[:, 2 * (j % 2) + t, 0:job.width],
                                             a[:, kt, t * P:(t + 1) * P], b[:, slot, kk, 0:job.width],
                                             start=(kt == 0 and a is hi and b is w_hi),
                                             stop=(kt == job.kts - 1 and a is lo))
                return last

            def iteration(phase, i, prev):
                for n, slot, u, j, job, k in iteration_units(phase, i):
                    if phase is PHASES[-1] and u >= len(phase.units) - RING:
                        continue
                    if k == 0 and prev is not None:
                        pe.wait_ge(acc_read, job_number(phase, i, j) - 1)
                    ready_operand(phase, i, prev, j, k)
                    pe.wait_ge(split_done, n + 1)
                    products(slot, j, job, k, range(TT)).then_inc(unit_used, 1)
                    after_unit(phase, i, prev, u)

            def last_units(phase):
                for t in range(TT):
                    for n, slot, u, j, job, k in list(iteration_units(phase, 0))[-RING:]:
                        if t == 0:
                            pe.wait_ge(split_done, n + 1)
                        last = products(slot, j, job, k, (t,))
                    last.then_inc(last_sums, 1)

            pe.wait_ge(ident_set, 1)
            pe.wait_ge(mem_gain_in, 16)
            turn(att[:, 3, 0:KD], mem_gain_rows[:]).then_inc(vecs_turned, 1)
            start_group(0)
            start_group(1)
            pe.wait_ge(consts, 1)
            run_phases(pe, iteration)
            last_units(PHASES[-1])

        @block.scalar
        def _(act):
            def round_unit(n, slot, number, width, first):
                act.wait_ge(raw_full[slot], number * 16)
                if not first:
                    act.wait_ge(unit_used, n - (RING - 1))
                act.activation(w_hi[:, slot, :, 0:width], w_raw[:, slot, :, 0:width], ACT.Copy).then_inc(hi_done, 1)

            def start_group(g):
                if g == KD // 2:
                    act.wait_ge(vecs_done, 2)
                act.wait_ge(start_turned, g + 1)
                hi = mem_hi if g < KD // 2 else u_hi
                for k in range(2):
                    kt = (2 * g + k) % KD
                    gain = (V_MEM if g < KD // 2 else V_MIX) + kt
                    last = act.activation(hi[:, kt, :], att[:, g % 3, k * SEQ:(k + 1) * SEQ], ACT.Copy,
                                          scale=vec[:, gain:gain + 1])
                last.then_inc(start_hi, 1)

            def square_start(which, c):
                src, here = ((mem_in, mem_here), (x_in, x_here))[which]
                act.wait_ge(here[c], 16)
                if c == 0 and not which:
                    act.wait_ge(mem_first, 16)
                if which:
                    act.wait_ge(squared, TT * NT)
                for t in range(TT):
                    act.activation(squares[:, c * TT + t, :], src[:, t, c * NCOL:(c + 1) * NCOL], ACT.Square,
                                   accum_out=ssq[:, which, t, c:c + 1]).then_inc(squared, 1)

            def root(which):
                act.wait_ge(mean_sq, which + 1)
                act.activation(rstd[:, which, :], rstd[:, which, :], ACT.Sqrt).then_inc(rooted, 1)

            def small_round():
                act.wait_ge(small_here, 32)
                act.activation(small_hi[:], small_raw[:], ACT.Copy).then_inc(small_hi_done, 1)

            def small_log():
                act.wait_ge(small_dve, 2)
                act.activation(z_abs[:], z_abs[:], ACT.Exp, scale=-1.0).then_inc(small_act, 1)
                act.wait_ge(small_act, 1)
                act.activation(z_abs[:], z_abs[:], ACT.Ln, bias=1.0).then_inc(small_act, 1)

            def small_floor():
                act.wait_ge(small_pe, 4)
                act.activation(floor_col[:], att[:, 2, 0:TT * ML_H].rearrange("p (t h) -> p t h", t=TT), ACT.Exp,
                               scale=-1.0).then_inc(small_act, 1)

            def mem_k(a):
                act.wait_ge(step_pe["mem"], pe_steps("mem", a, 1))
                act.activation(buf_x[:, 2:4, 0:SEQ], att[:, 1, :].rearrange("p (d t) -> p d t", d=2),
                               ACT.Copy).then_inc(step_act["mem"], 1)

            def mem_exp(a):
                act.wait_ge(step_dve["mem"], dve_steps("mem", a, 2))
                for t in range(TT):
                    act.activation(buf_p[:, t, :], att[:, 2, t * MEM_LEN:(t + 1) * MEM_LEN], ACT.Exp,
                                   bias=stat[:, 0, t:t + 1], accum_out=stat[:, 1, t:t + 1]
                                   ).then_inc(step_act["mem"], 1)

            def mem_y(a):
                act.wait_ge(step_pe["mem"], pe_steps("mem", a, 4))
                act.activation(y["mem"][0][:, bass.ds(a * 2, 2), :], att[:, 1, :].rearrange("p (e t) -> p e t", e=2),
                               ACT.Copy).then_inc(y_hi["mem"], 1)

            def ml_pad(a):
                act.wait_ge(step_pe["ml"], pe_steps("ml", a, 1))
                for b in range(2):
                    act.activation(buf_x[:, 2 * b:2 * b + 2, 3:3 + SEQ],
                                   att[:, b, :].rearrange("p (d t) -> p d t", d=2), ACT.Copy
                                   ).then_inc(step_act["ml"], 1)

            def ml_sigmoids(a):
                act.wait_ge(step_dve["ml"], dve_steps("ml", a, 1))
                act.activation(buf_t[:], buf_p[:], ACT.Sigmoid).then_inc(step_act["ml"], 1)

            def ml_output_gate(a):
                act.activation(buf_b[:, :, 1, 0:GC], buf_b[:, :, 1, 0:GC], ACT.Sigmoid)

            def ml_exp(a):
                act.wait_ge(step_dve["ml"], dve_steps("ml", a, 3))
                act.activation(buf_p[:, 0:2, :].rearrange("p a b -> p (a b)")[:, 0:3 * P],
                               buf_p[:, 0:2, :].rearrange("p a b -> p (a b)")[:, 0:3 * P], ACT.Exp,
                               scale=-1.0).then_inc(step_act["ml"], 1)

            def ml_square(a):
                act.wait_ge(step_dve["ml"], dve_steps("ml", a, 5))
                for t in range(TT):
                    act.activation(buf_t[:, t, :], att[:, t, 0:GC], ACT.Square, scale=stat[:, 2, t:t + 1],
                                   accum_out=stat[:, 1, t:t + 1]).then_inc(step_act["ml"], 1)
                act.wait_ge(step_act["ml"], act_steps("ml", a, 6))
                act.activation(stat[:, 3, 0:2], stat[:, 1, 0:2], ACT.Sqrt, scale=1.0 / ML_D,
                               bias=eps[:, 0:1]).then_inc(step_act["ml"], 1)

            def ml_y(a):
                act.wait_ge(step_pe["ml"], pe_steps("ml", a, 4))
                for e in range(2):
                    last = act.activation(y["ml"][0][:, bass.ds(a * 2 + e, 1), :].rearrange("p a t -> p (a t)"),
                                          att[:, 2, e * SEQ:(e + 1) * SEQ],
                                          ACT.Copy, scale=ml_gain[:, bass.ds(a * 2 + e, 1)])
                last.then_inc(y_hi["ml"], 1)

            def fox_qk(a):
                act.wait_ge(step_pe["fox"], pe_steps("fox", a, 1))
                act.activation(buf_x[:, 2, 0:SEQ], att[:, 1, 0:SEQ], ACT.Copy, scale=FOX_D ** -0.5)
                act.activation(buf_x[:, 3, 0:SEQ], att[:, 1, SEQ:2 * SEQ], ACT.Copy).then_inc(step_act["fox"], 1)

            def fox_exp(a):
                act.wait_ge(step_dve["fox"], dve_steps("fox", a, 3))
                for h in range(2):
                    p_h = buf_p[:, 2 * h:2 * h + 2, :].rearrange("p a b -> p (a b)")
                    for t, cols in ((0, slice(0, P)), (1, slice(P, 3 * P))):
                        c = 2 * h + t
                        last = act.activation(p_h[:, cols], p_h[:, cols], ACT.Exp, bias=stat[:, 0, c:c + 1],
                                              accum_out=stat[:, 1, c:c + 1])
                    last.then_inc(step_act["fox"], 1)

            def fox_p(a):
                act.wait_ge(step_pe["fox"], pe_steps("fox", a, 4))
                act.activation(buf_t[:, 2:4, :].rearrange("p a b -> p (a b)")[:, 0:3 * P], att[:, 1, 0:3 * P],
                               ACT.Copy).then_inc(step_act["fox"], 1)

            def fox_y(a):
                act.wait_ge(step_pe["fox"], pe_steps("fox", a, 5))
                act.activation(y["fox"][0][:, bass.ds(a * 2, 2), :], att[:, 2, :].rearrange("p (e t) -> p e t", e=2),
                               ACT.Copy).then_inc(y_hi["fox"], 1)

            def tile_hi_part(dst, kt0, q, gain=None):
                for b in range(2):
                    act.wait_ge(tile_turned, q * 2 + b + 1)
                    if gain is None:
                        last = act.activation(dst[:, bass.ds(kt0 + 2 * b, 2), :],
                                              att[:, b, :].rearrange("p (k t) -> p k t", k=2), ACT.Copy)
                    else:
                        for k in range(2):
                            kt = kt0 + 2 * b + k
                            last = act.activation(dst[:, kt, :], att[:, b, k * SEQ:(k + 1) * SEQ], ACT.Copy,
                                                  scale=vec[:, gain + kt:gain + kt + 1])
                    last.then_inc(tile_hi, 1)

            def square_tile(which, n, ready):
                act.wait_ge(ready[0], ready[1])
                for t in range(TT):
                    act.activation(scratch[:], res[:, t, n * NCOL:(n + 1) * NCOL], ACT.Square,
                                   accum_out=ssq[:, which, t, n:n + 1]).then_inc(squared, 1)
                    act.wait_ge(squared, which * TT * NT + n * TT + t + 1)

            ATTENTION = {"mem": {0: mem_k, 2: mem_exp, 6: mem_y},
                         "ml": {0: ml_pad, 3: ml_sigmoids, 4: ml_output_gate, 6: ml_exp, 10: ml_square, 13: ml_y},
                         "fox": {0: fox_qk, 3: fox_exp, 7: fox_p, 10: fox_y}}

            def after_unit(phase, i, prev, u, n):
                last_of_job = u + 1 == len(phase.units) or phase.units[u + 1][1] == 0
                if prev is None:
                    if EARLY + u < KD:
                        start_group(EARLY + u)
                    if 1 <= u < 1 + NT:
                        square_start(0, u - 1)
                    if u == 6:
                        root(0)
                    if 5 <= u < 5 + NT:
                        square_start(1, u - 5)
                    if u == 10:
                        root(1)
                elif prev.name in ATTENTION:
                    if u in ATTENTION[prev.name]:
                        ATTENTION[prev.name][u](GROUPS - 1 if peeled(i) else i - 1)
                if phase.name == "ml" and prev.name == "mem":
                    for at_unit, do in ((0, small_round), (5, small_log), (11, small_floor)):
                        if u == at_unit:
                            do()
                if phase.name == "merge":
                    if u == 1 and prev.name == "merge":
                        tile_hi_part(merged_hi, (i - 1) * 4, i - 1)
                    if last_of_job and phase.units[u][0] % 2 == 0:
                        j = phase.units[u][0] // 2
                        act.wait_ge(acc_read, job_number(phase, i, 2 * j) + 1)
                        act.activation(gate[:], gate[:], ACT.Sigmoid).then_inc(gate_done, 1)
                if phase.name == "out":
                    j = u // (KD // UK)
                    if u % (KD // UK) == 1:
                        if j == 0:
                            tile_hi_part(merged_hi, (NT - 1) * 4, NT - 1)
                        else:
                            tile_hi_part(u_hi, (j - 1) * 4, NT + j - 1, V_FFN)
                    if last_of_job:
                        square_tile(2, j, (acc_read, job_number(phase, i, j) + 1))
                if phase.name in ("ffn_a", "ffn_b"):
                    if u == 1:
                        if prev.name == "out":
                            tile_hi_part(u_hi, (NT - 1) * 4, 2 * NT - 1, V_FFN)
                        elif prev is phase:
                            tile_hi_part(h_hi, (i - 1) * 4, i + (TILE0[phase.name] - 1))
                    if prev.name == "out" and u == 3:
                        root(2)
                    if last_of_job and phase.units[u][0] == 0:
                        act.wait_ge(unit_used, n + 1)
                        act.wait_ge(rstd_done, 3)
                        for t in range(TT):
                            act.activation(gate[:, t, :], acc[:, t, :], ACT.Sigmoid,
                                           scale=rstd[:, 2, t:t + 1]).then_inc(ffn_sig, 1)
                if phase.name in ("down_a", "down_b"):
                    if u == 1:
                        tiles = FT_A if phase.name == "down_a" else FT - FT_A
                        q = TILE0["ffn_a"] + (FT_A if phase.name == "down_a" else FT) - 1
                        tile_hi_part(h_hi, (tiles - 1) * 4, q)
                    if u == 2 and phase.name == "down_b":
                        act.activation(warm[:, 1:2], eps[:], ACT.Sqrt)
                    if last_of_job and phase.name == "down_b" and phase.units[u][0] < NT - 1:
                        j = phase.units[u][0]
                        square_tile(3, j, (acc_read, job_number(phase, i, j) + 1))

            def loads_of_slot(phase, i, u):
                s, per = u % RING, len(phase.units)
                if u >= per and phase.iters == 1:
                    following = PHASES[PHASES.index(phase) + 1]
                    return following.loads0[s] + following.jobs[0].loads
                before = phase.loads0[s] + phase.per_slot[s] * (u // per)
                return i * phase.per_slot[s] + (before + sum(phase.jobs[j].loads for j, _ in
                                                             phase.units[s:u % per + 1:RING]))

            def ahead(phase, i, u):
                m = u + LEAD
                per = len(phase.units)
                if m < per:
                    width = phase.jobs[phase.units[m][0]].width
                else:
                    if phase is PHASES[-1] and m >= per:
                        return
                    width = NCOL
                round_unit(i * per + (phase.unit0 + m), m % RING, loads_of_slot(phase, i, m), width,
                           phase.unit0 == 0 and peeled(i) and m < RING)

            def iteration(phase, i, prev):
                for n, slot, u, j, job, k in iteration_units(phase, i):
                    ahead(phase, i, u)
                    after_unit(phase, i, prev, u, n)

            act.wait_ge(eps_set, 1)
            act.activation(warm[:, 0:1], eps[:], ACT.Sqrt)
            act.wait_ge(vecs_done, 1)
            for u in range(LEAD):
                if u < EARLY:
                    start_group(u)
                round_unit(u, u, PHASES[0].jobs[0].loads, NCOL, True)
            run_phases(act, iteration)
            for t in range(TT):
                act.wait_ge(last_res, t + 1)
                act.activation(scratch[:], res[:, t, (NT - 1) * NCOL:], ACT.Square,
                               accum_out=ssq[:, 3, t, NT - 1:NT]).then_inc(squared, 1)
                act.wait_ge(mean_sq, 3 + t + 1)
                act.activation(rstd[:, 3, t:t + 1], rstd[:, 3, t:t + 1], ACT.Sqrt).then_inc(rooted, 1)
                act.wait_ge(rstd_done, 3 + t + 1)
                act.wait_ge(gained, NT - 1)
                for n in (1, 2):
                    act.activation(res[:, t, n * NCOL:(n + 1) * NCOL], res[:, t, n * NCOL:(n + 1) * NCOL], ACT.Copy,
                                   scale=rstd[:, 3, t:t + 1]).then_inc(final_act, 1)

        @block.vector
        def _(dve):
            chain = Chain(dve, dve_order, LINKS)
            link = chain.link

            def split_unit(n, slot, width):
                dve.wait_ge(hi_done, n + 1)
                dve.tensor_tensor(w_lo[:, slot, :, 0:width], w_raw[:, slot, :, 0:width],
                                  w_hi[:, slot, :, 0:width].bitcast(F32), ALU.subtract).then_inc(split_done, 1)

            def start_group(g):
                dve.wait_ge(start_hi, g + 1)
                hi, lo = (mem_hi, mem_lo) if g < KD // 2 else (u_hi, u_lo)
                for k in range(2):
                    kt = (2 * g + k) % KD
                    gain = (V_MEM if g < KD // 2 else V_MIX) + kt
                    last = dve.scalar_tensor_tensor(lo[:, kt, :], att[:, g % 3, k * SEQ:(k + 1) * SEQ],
                                                    vec[:, gain:gain + 1], hi[:, kt, :].bitcast(F32),
                                                    ALU.mult, ALU.subtract)
                last.then_inc(start_lo, 1)

            def copy_vectors():
                dve.wait_ge(vecs_turned, 2)
                dve.tensor_copy(vec[:, 0:VR], att[:, 3, 0:VR])
                dve.tensor_copy(ml_gain[:], att[:, 3, VR:VR + KW]).then_inc(vecs_done, 1)
                dve.wait_ge(vecs_done, 2)

            def mean_square(which):
                dve.wait_ge(squared, (which + 1) * TT * NT)
                link(dve.tensor_reduce(rstd[:, which, :], ssq[:, which, :, :], AX_X, ALU.add))
                dve.tensor_scalar(rstd[:, which, :], rstd[:, which, :], 1.0 / D, EPS, ALU.mult, ALU.add
                                  ).then_inc(mean_sq, 1)

            def invert(which):
                dve.wait_ge(rooted, which + 1)
                dve.reciprocal(rstd[:, which, :], rstd[:, which, :]).then_inc(rstd_done, 1)
                dve.wait_ge(rstd_done, which + 1)

            def small_remainder():
                dve.wait_ge(small_hi_done, 1)
                dve.tensor_tensor(small_lo[:], small_raw[:], small_hi[:].bitcast(F32), ALU.subtract
                                  ).then_inc(small_split, 1)

            def small_copy():
                dve.wait_ge(small_pe, 1)
                dve.tensor_copy(small_rows[:], att[0:SMALL, 3, 0:SEQ]).then_inc(small_dve, 1)

            def small_logits():
                dve.wait_ge(small_pe, 2)
                dve.wait_ge(small_bias_here, 32)
                for t in range(TT):
                    last = dve.scalar_tensor_tensor(z[:, t, :], att[:, 3, t * SMALL:(t + 1) * SMALL],
                                                    rstd[:, 1, t:t + 1], small_bias[:], ALU.mult, ALU.add)
                link(last)
                dve.scalar_tensor_tensor(z_abs[:], z[:], -1.0, z[:], ALU.mult, ALU.max).then_inc(small_dve, 1)

            def small_log_sigmoid():
                dve.wait_ge(small_act, 2)
                dve.scalar_tensor_tensor(log_sig[:], z[:], 0.0, z_abs[:], ALU.min, ALU.subtract
                                         ).then_inc(small_dve, 1)

            def small_scans():
                dve.wait_ge(small_pe, 3)
                dve.tensor_tensor_scan(f_fox[:], ones_row[:], att[0:FOX_H, 3, 0:SEQ], 0.0, ALU.mult, ALU.add)
                link(dve.tensor_tensor_scan(f_ml[:], ones_row[0:ML_H, :], att[0:ML_H, 2, 0:SEQ], 0.0,
                                            ALU.mult, ALU.add))
                link(dve.tensor_tensor(a_ml[:], att[0:ML_H, 3, SEQ:2 * SEQ], f_ml[:], ALU.subtract))
                link(dve.tensor_tensor_scan(m_ml[:], ones_row[0:ML_H, :], a_ml[:], 0.0, ALU.mult, ALU.max))
                dve.tensor_tensor(fm_ml[:], f_ml[:], m_ml[:], ALU.add).then_inc(small_dve, 1)

            def small_columns():
                dve.wait_ge(small_pe, 4)
                dve.tensor_copy(a_col[:], att[:, 3, 0:TT * ML_H].rearrange("p (t h) -> p t h", t=TT)
                                ).then_inc(small_dve, 1)

            def y_lo(b, a):
                dve.wait_ge(y_hi[b], a + 1)
                bank = 1 if b == "mem" else 2
                dve.tensor_tensor(y[b][1][:, bass.ds(a * 2, 2), :], att[:, bank, :].rearrange("p (e t) -> p e t", e=2),
                                  y[b][0][:, bass.ds(a * 2, 2), :].bitcast(F32), ALU.subtract
                                  ).then_inc(y_done[b], 1)

            def mem_q(a):
                dve.wait_ge(step_pe["mem"], pe_steps("mem", a, 1))
                dve.tensor_scalar(buf_x[:, 0:2, 0:SEQ], att[:, 0, :].rearrange("p (d t) -> p d t", d=2),
                                  MEM_D ** -0.5, None, ALU.mult).then_inc(step_dve["mem"], 1)

            def mem_max(a):
                dve.wait_ge(step_pe["mem"], pe_steps("mem", a, 2))
                link(dve.tensor_reduce(stat[:, 2, 0:2], att[:, 2, :].rearrange("p (t m) -> p t m", t=TT), AX_X,
                                       ALU.max))
                dve.tensor_scalar(stat[:, 0, 0:2], stat[:, 2, 0:2], -1.0, None, ALU.mult
                                  ).then_inc(step_dve["mem"], 1)
                dve.wait_ge(step_act["mem"], act_steps("mem", a, 3))
                link(dve.reciprocal(stat[:, 2, 0:2], stat[:, 1, 0:2]))
                for t in range(TT):
                    last = dve.tensor_scalar(buf_p[:, t, :], buf_p[:, t, :], stat[:, 2, t:t + 1], None, ALU.mult)
                last.then_inc(step_dve["mem"], 1)

            def mem_p(a):
                dve.wait_ge(step_pe["mem"], pe_steps("mem", a, 3))
                dve.tensor_copy(buf_t[:, 0:2, :], att[:, 0, :].rearrange("p (m t) -> p m t", m=2)
                                ).then_inc(step_dve["mem"], 1)

            def mem_y(a):
                y_lo("mem", a)

            def conv_tap(a, tap):
                for g in range(4):
                    c = (g // 2) * KW + g % 2
                    w_tap = vec[:, bass.ds(a * 2 + (V_CW + tap * KD + c), 1)]
                    if tap == 3:
                        last = dve.tensor_scalar(buf_p[:, g, :], buf_x[:, g, tap:tap + SEQ], w_tap,
                                                 vec[:, bass.ds(a * 2 + (V_CB + c), 1)], ALU.mult, ALU.add)
                    else:
                        last = dve.scalar_tensor_tensor(buf_p[:, g, :], buf_x[:, g, tap:tap + SEQ], w_tap,
                                                        buf_p[:, g, :], ALU.mult, ALU.add)
                return last

            def ml_conv_1(a):
                dve.wait_ge(step_act["ml"], act_steps("ml", a, 2))
                link(conv_tap(a, 3))
                link(conv_tap(a, 2))

            def ml_conv_2(a):
                link(conv_tap(a, 1))

            def ml_conv_3(a):
                conv_tap(a, 0).then_inc(step_dve["ml"], 1)

            def ml_silu(a):
                dve.tensor_scalar(buf_f[0:ML_H, 0, :], m_ml[:], ident[0:ML_H, bass.ds(a, 1)], None, ALU.mult)
                dve.wait_ge(step_act["ml"], act_steps("ml", a, 3))
                dve.tensor_tensor(buf_t[:, 0:2, :], buf_p[:, 0:2, :], buf_t[:, 0:2, :], ALU.mult)
                dve.scalar_tensor_tensor(buf_t[:, 2:4, :], buf_p[:, 2:4, :], ML_D ** -0.5, buf_t[:, 2:4, :],
                                         ALU.mult, ALU.mult).then_inc(step_dve["ml"], 1)

            def ml_weights(a):
                dve.wait_ge(step_pe["ml"], pe_steps("ml", a, 2))
                e = buf_p[:, 0:2, :].rearrange("p a b -> p (a b)")
                dve.tensor_scalar(e[:, 0:SEQ], att[:, 3, 0:SEQ], a_col[:, 0, bass.ds(a, 1)], 0.0,
                                  ALU.subtract, ALU.max)
                dve.tensor_scalar(e[:, SEQ:SEQ + P], att[:, 3, P:SEQ], a_col[:, 1, bass.ds(a, 1)], 0.0,
                                  ALU.subtract, ALU.max).then_inc(step_dve["ml"], 1)
                dve.wait_ge(step_act["ml"], act_steps("ml", a, 4))
                dve.tensor_tensor(e[:, 0:P], e[:, 0:P], mask_mul[:], ALU.mult)
                link(dve.tensor_tensor(e[:, SEQ:SEQ + P], e[:, SEQ:SEQ + P], mask_mul[:], ALU.mult))
                p_t = buf_p[:, 2:4, :].rearrange("p a b -> p (a b)")
                dve.tensor_tensor(p_t[:, 0:3 * P], att[:, 2, 0:3 * P], e[:, 0:3 * P], ALU.mult
                                  ).then_inc(step_dve["ml"], 1)

            def ml_denominator(a):
                dve.wait_ge(step_pe["ml"], pe_steps("ml", a, 3))
                for t in range(TT):
                    last = dve.tensor_scalar(stat[:, 0, t:t + 1], att[:, t, GC:GC + 1],
                                             floor_col[:, t, bass.ds(a, 1)], None, ALU.max)
                link(last)
                for t in range(TT):
                    last = dve.scalar_tensor_tensor(stat[:, 0, t:t + 1], att[:, t, GC:GC + 1], -1.0,
                                                    stat[:, 0, t:t + 1], ALU.mult, ALU.max)
                link(last)
                dve.reciprocal(stat[:, 2, 0:2], stat[:, 0, 0:2]).then_inc(step_dve["ml"], 1)

            def ml_output(a):
                dve.wait_ge(step_act["ml"], act_steps("ml", a, 7))
                link(dve.reciprocal(stat[:, 0, 0:2], stat[:, 3, 0:2]))
                link(dve.tensor_tensor(stat[:, 0, 2:4], stat[:, 0, 0:2], stat[:, 2, 0:2], ALU.mult))
                for t in range(TT):
                    last = dve.scalar_tensor_tensor(buf_y[:, t, :], att[:, t, 0:GC], stat[:, 0, 2 + t:3 + t],
                                                    buf_b[:, t, 1, 0:GC], ALU.mult, ALU.mult)
                last.then_inc(step_dve["ml"], 1)

            def ml_y(a):
                dve.wait_ge(y_hi["ml"], a + 1)
                for e in range(2):
                    last = dve.scalar_tensor_tensor(
                        y["ml"][1][:, bass.ds(a * 2 + e, 1), :].rearrange("p a t -> p (a t)"),
                        att[:, 2, e * SEQ:(e + 1) * SEQ], ml_gain[:, bass.ds(a * 2 + e, 1)],
                        y["ml"][0][:, bass.ds(a * 2 + e, 1), :].rearrange("p a t -> p (a t)").bitcast(F32),
                        ALU.mult, ALU.subtract)
                last.then_inc(y_done["ml"], 1)

            def fox_qk(a):
                for h in range(2):
                    last = dve.tensor_scalar(buf_f[:, h, :], f_fox[:], ident[0:FOX_H, bass.ds(a * 2 + h, 1)], None,
                                             ALU.mult)
                last.then_inc(step_dve["fox"], 1)
                dve.wait_ge(step_pe["fox"], pe_steps("fox", a, 1))
                dve.tensor_scalar(buf_x[:, 0, 0:SEQ], att[:, 0, 0:SEQ], FOX_D ** -0.5, None, ALU.mult)
                dve.tensor_copy(buf_x[:, 1, 0:SEQ], att[:, 0, SEQ:2 * SEQ]).then_inc(step_dve["fox"], 1)

            def fox_max(a):
                for h in range(2):
                    dve.wait_ge(step_pe["fox"], pe_steps("fox", a, 2 + h))
                    p_h = buf_p[:, 2 * h:2 * h + 2, :].rearrange("p a b -> p (a b)")
                    link(dve.tensor_tensor(p_h[:, 0:3 * P], att[:, 2 + h, 0:3 * P],
                                           mask_add[:].rearrange("p a b -> p (a b)"), ALU.add))
                    dve.tensor_reduce(stat[:, 2, 2 * h:2 * h + 1], p_h[:, 0:P], AX_X, ALU.max)
                    last = dve.tensor_reduce(stat[:, 2, 2 * h + 1:2 * h + 2], p_h[:, P:3 * P], AX_X, ALU.max)
                    link(last)
                dve.tensor_scalar(stat[:, 0, :], stat[:, 2, :], -1.0, None, ALU.mult
                                  ).then_inc(step_dve["fox"], 1)
                dve.wait_ge(step_act["fox"], act_steps("fox", a, 3))
                link(dve.reciprocal(stat[:, 2, :], stat[:, 1, :]))
                for h in range(2):
                    p_h = buf_p[:, 2 * h:2 * h + 2, :].rearrange("p a b -> p (a b)")
                    for t, cols in ((0, slice(0, P)), (1, slice(P, 3 * P))):
                        c = 2 * h + t
                        last = dve.tensor_scalar(p_h[:, cols], p_h[:, cols], stat[:, 2, c:c + 1], None, ALU.mult)
                last.then_inc(step_dve["fox"], 1)

            def fox_p(a):
                dve.wait_ge(step_pe["fox"], pe_steps("fox", a, 4))
                dve.tensor_copy(buf_t[:, 0:2, :].rearrange("p a b -> p (a b)")[:, 0:3 * P], att[:, 0, 0:3 * P]
                                ).then_inc(step_dve["fox"], 1)

            def fox_y(a):
                y_lo("fox", a)

            def tile_lo_part(hi, lo, kt0, q, gain=None):
                for b in range(2):
                    dve.wait_ge(tile_hi, q * 2 + b + 1)
                    if gain is None:
                        last = dve.tensor_tensor(lo[:, bass.ds(kt0 + 2 * b, 2), :],
                                                 att[:, b, :].rearrange("p (k t) -> p k t", k=2),
                                                 hi[:, bass.ds(kt0 + 2 * b, 2), :].bitcast(F32), ALU.subtract)
                    else:
                        for k in range(2):
                            kt = kt0 + 2 * b + k
                            last = dve.scalar_tensor_tensor(lo[:, kt, :], att[:, b, k * SEQ:(k + 1) * SEQ],
                                                            vec[:, gain + kt:gain + kt + 1],
                                                            hi[:, kt, :].bitcast(F32), ALU.mult, ALU.subtract)
                    last.then_inc(tile_lo, 1)

            ATTENTION = {"mem": {0: mem_q, 2: mem_max, 4: mem_p, 6: mem_y},
                         "ml": {0: ml_conv_1, 1: ml_conv_2, 2: ml_conv_3, 4: ml_silu, 6: ml_weights, 9: ml_denominator,
                                10: ml_output, 13: ml_y},
                         "fox": {0: fox_qk, 3: fox_max, 7: fox_p, 10: fox_y}}

            def finish_job(phase, i, prev, j, n):
                job = phase.jobs[j]
                bank = 2 * (j % 2)
                number = job_number(phase, i, j)
                dve.wait_ge(unit_used, n + 1)
                if not (peeled(i) and phase.job0 == 0 and j == 0):
                    dve.wait_ge(acc_read, number)
                b = bias_of(phase, j)
                if b:
                    slot, load = bias_number(phase, i, j)
                    dve.wait_ge(bias_full[slot], load * 16 + 16)
                if phase.name in ATTENTION:
                    if prev is not None:
                        a = GROUPS - 1 if peeled(i) else i - 1
                        steps = {"mem": (4, 1), "ml": (1, 3), "fox": (1, 5)}[prev.name][j]
                        dve.wait_ge(step_pe[prev.name], pe_steps(prev.name, a, steps))
                    for t in range(TT):
                        src = acc[:, bank + t, 0:job.width]
                        dst = buf_a[:, t, :] if j == 0 else buf_b[:, t, 0, 0:GC]
                        bb = bias[:, b[0], 0:job.width] if b else None
                        if phase.name == "ml" and j == 1:
                            dst = buf_b[:, t, :, 0:GC]
                            src = src.rearrange("p (g c) -> p g c", g=2)
                            bb = bb.rearrange("p (g c) -> p g c", g=2)
                        if b:
                            last = dve.scalar_tensor_tensor(dst, src, rstd[:, 1, t:t + 1], bb, ALU.mult, ALU.add)
                        else:
                            last = dve.tensor_scalar(dst, src, rstd[:, 0, t:t + 1], None, ALU.mult)
                elif phase.name == "merge" and j % 2 == 0:
                    for t in range(TT):
                        last = dve.scalar_tensor_tensor(gate[:, t, :], acc[:, bank + t, :], rstd[:, 1, t:t + 1],
                                                        bias[:, b[0], :], ALU.mult, ALU.add)
                elif phase.name == "merge":
                    dve.wait_ge(gate_done, i * 3 + (j // 2 + 1))
                    if j == 1 and not peeled(i):
                        dve.wait_ge(tile_turned, i * 2)
                    for t in range(TT):
                        if j == 1:
                            last = dve.tensor_tensor(merged[:, t, :], acc[:, bank + t, :], gate[:, t, :], ALU.mult)
                        else:
                            link(dve.tensor_tensor(scratch[:], acc[:, bank + t, :], gate[:, t, :], ALU.mult))
                            last = dve.tensor_tensor(merged[:, t, :], merged[:, t, :], scratch[:], ALU.add)
                            if t + 1 < TT:
                                link(last)
                elif phase.name in ("out", "down_a", "down_b"):
                    if phase.name == "out" and j == 0:
                        dve.wait_ge(res_here, 16)
                    cols = slice(j * NCOL, (j + 1) * NCOL)
                    for t in range(TT):
                        last = dve.tensor_tensor(res[:, t, cols], acc[:, bank + t, :], res[:, t, cols], ALU.add)
                elif j == 0:
                    tiles = 0 if phase.name == "ffn_a" else FT_A
                    for t in range(TT):
                        dve.wait_ge(ffn_sig, i * TT + (tiles * TT + t + 1))
                        last = dve.scalar_tensor_tensor(merged[:, t, :], acc[:, bank + t, :], rstd[:, 2, t:t + 1],
                                                        gate[:, t, :], ALU.mult, ALU.mult)
                else:
                    dve.wait_ge(tile_turned, i * 2 + 2 * TILE0[phase.name])
                    for t in range(TT):
                        last = dve.scalar_tensor_tensor(buf_a[:, t, :], acc[:, bank + t, :], rstd[:, 2, t:t + 1],
                                                        merged[:, t, :], ALU.mult, ALU.mult)
                last.then_inc(acc_read, 1)

            def after_unit(phase, i, prev, u, n):
                if prev is None and u == 7:
                    invert(0)
                if prev is None and u == 15:
                    invert(1)
                if u + 1 == len(phase.units) and phase is PHASES[-1]:
                    return
                if u + 1 == len(phase.units) or phase.units[u + 1][1] == 0:
                    finish_job(phase, i, prev, phase.units[u][0], n)
                if prev is None:
                    if EARLY + u < KD:
                        start_group(EARLY + u)
                    if u == 3:
                        copy_vectors()
                    if u == 5:
                        mean_square(0)
                    if u == 9:
                        mean_square(1)
                elif prev.name in ATTENTION and u in ATTENTION[prev.name]:
                    ATTENTION[prev.name][u](GROUPS - 1 if peeled(i) else i - 1)
                if phase.name == "ml" and prev.name == "mem":
                    for at_unit, do in ((0, small_remainder), (1, small_copy), (3, small_logits),
                                        (6, small_log_sigmoid),
                                        (8, small_scans), (11, small_columns)):
                        if u == at_unit:
                            do()
                    if u == 12:
                        dve.memset(buf_x[:, :, 0:3], 0.0)
                if phase.name == "merge" and prev is phase and u == 1:
                    tile_lo_part(merged_hi, merged_lo, (i - 1) * 4, i - 1)
                if phase.name == "out" and u % (KD // UK) == 1:
                    j = u // (KD // UK)
                    if j == 0:
                        tile_lo_part(merged_hi, merged_lo, (NT - 1) * 4, NT - 1)
                    else:
                        tile_lo_part(u_hi, u_lo, (j - 1) * 4, NT + j - 1, V_FFN)
                if phase.name in ("ffn_a", "ffn_b") and u == 1:
                    if prev.name == "out":
                        tile_lo_part(u_hi, u_lo, (NT - 1) * 4, 2 * NT - 1, V_FFN)
                        mean_square(2)
                    elif prev is phase:
                        tile_lo_part(h_hi, h_lo, (i - 1) * 4, i + (TILE0[phase.name] - 1))
                if phase.name == "ffn_a" and prev.name == "out" and u == 4:
                    invert(2)
                j, k = phase.units[u]
                if phase.name == "down_b" and j > 0 and k == 5:
                    dve.wait_ge(final_here, 16)
                    dve.wait_ge(squared, 3 * TT * NT + j * TT)
                    cols = slice((j - 1) * NCOL, j * NCOL)
                    for t in range(TT):
                        last = dve.tensor_tensor(res[:, t, cols], res[:, t, cols], g_final[:, cols], ALU.mult)
                    last.then_inc(gained, 1)
                if phase.name in ("down_a", "down_b") and u == 1:
                    tiles = FT_A if phase.name == "down_a" else FT - FT_A
                    q = TILE0["ffn_a"] + (FT_A if phase.name == "down_a" else FT) - 1
                    tile_lo_part(h_hi, h_lo, (tiles - 1) * 4, q)

            def ahead(phase, i, u):
                m = u + LEAD
                per = len(phase.units)
                if m >= per and phase is PHASES[-1]:
                    return
                width = phase.jobs[phase.units[m][0]].width if m < per else NCOL
                split_unit(i * per + (phase.unit0 + m), m % RING, width)

            def iteration(phase, i, prev):
                for n, slot, u, j, job, k in iteration_units(phase, i):
                    ahead(phase, i, u)
                    after_unit(phase, i, prev, u, n)

            dve.wait_ge(vecs_turned, 1)
            dve.tensor_copy(vec[:, V_MEM:V_MEM + KD], att[:, 3, 0:KD]).then_inc(vecs_done, 1)
            dve.wait_ge(vecs_done, 1)
            for u in range(LEAD):
                if u < EARLY:
                    start_group(u)
                split_unit(u, u, NCOL)
            run_phases(dve, iteration, chain)
            last_cols = slice((NT - 1) * NCOL, NT * NCOL)
            for t in range(TT):
                dve.wait_ge(last_sums, t + 1)
                dve.tensor_tensor(res[:, t, last_cols], acc[:, 2 * ((NT - 1) % 2) + t, :], res[:, t, last_cols], ALU.add
                                  ).then_inc(last_res, 1)
                dve.wait_ge(squared, 3 * TT * NT + (NT - 1) * TT + t + 1)
                link(dve.tensor_reduce(rstd[:, 3, t:t + 1], ssq[:, 3, t, :], AX_X, ALU.add))
                dve.tensor_scalar(rstd[:, 3, t:t + 1], rstd[:, 3, t:t + 1], 1.0 / D, EPS, ALU.mult, ALU.add
                                  ).then_inc(mean_sq, 1)
                dve.wait_ge(rooted, 3 + t + 1)
                dve.reciprocal(rstd[:, 3, t:t + 1], rstd[:, 3, t:t + 1]).then_inc(rstd_done, 1)
                dve.wait_ge(rstd_done, 3 + t + 1)
                dve.wait_ge(gained, NT - 1)
                dve.tensor_scalar(res[:, t, 0:NCOL], res[:, t, 0:NCOL], rstd[:, 3, t:t + 1], None, ALU.mult
                                  ).then_inc(final_dve, 1)
                dve.scalar_tensor_tensor(res[:, t, last_cols], res[:, t, last_cols], rstd[:, 3, t:t + 1],
                                         g_final[:, last_cols], ALU.mult, ALU.mult).then_inc(final_dve, 1)


def kernel(x, mem, norm_mix, w_in, b_in, conv_w, conv_b, mlstm_norm, norm_mem, w_mem_kv, w_br_fox,
           w_br_mlstm, w_br_mem, w_out, norm_ffn, w_ffn_in, w_ffn_out, norm_final):
    import numpy as np
    import concourse.bacc as bacc
    from concourse import mybir as mb
    from concourse.bass_utils import run_bass_kernel_spmd

    given = dict(x=x, mem=mem, norm_mix=norm_mix, w_in=w_in, b_in=b_in, conv_w=conv_w, conv_b=conv_b,
                 mlstm_norm=mlstm_norm, norm_mem=norm_mem, w_mem_kv=w_mem_kv, w_br_fox=w_br_fox,
                 w_br_mlstm=w_br_mlstm, w_br_mem=w_br_mem, w_out=w_out, norm_ffn=norm_ffn,
                 w_ffn_in=w_ffn_in, w_ffn_out=w_ffn_out, norm_final=norm_final)
    nc = bacc.Bacc("TRN2", target_bir_lowering=False, num_devices=1)
    arrays, args = {}, {}
    for name, value in given.items():
        a = np.ascontiguousarray(value)
        arrays["in_" + name] = a
        args[name] = nc.dram_tensor("in_" + name, a.shape, mb.dt.from_np(a.dtype), kind="ExternalInput").ap()
    out = nc.dram_tensor("out_y", (1, SEQ, D), mb.dt.float32, kind="ExternalOutput").ap()
    hybrid_layer(nc, out=out, **args)
    return run_bass_kernel_spmd(nc, [arrays], core_ids=[0]).results[0]["out_y"]
```
